# Optimizing a Trainium2 kernel written in Bass

```python
import jax, jax.numpy as jnp
from jax import lax
import numpy as np

D_MODEL = 1024
BATCH = 1
SEQ = 128
DEPTH = 2
DEC_BATCH = 1
DEC_SEQ = 512
PAST_LEN = 128

GRID_W = 64
EPS = 1e-6
N_EVEN = (DEPTH + 1) // 2
N_ODD = DEPTH // 2
HG_DK = 128
HG_DV = 128
HG_HEADS = (D_MODEL // 2) // HG_DV
HG_CHUNK = 64
HEAD_DIM = 64
N_HEADS = (D_MODEL // 2) // HEAD_DIM
KV_HEADS = 2
Q_PER_KV = N_HEADS // KV_HEADS
WINDOW = 128
ATT_BLOCK = 128
ROPE_BASE = 10000.0
NEG_INF = -1e30
EVEN_IN = 3 * HG_HEADS * HG_DK + 2 * HG_HEADS * HG_DV + N_HEADS * HEAD_DIM + 2 * KV_HEADS * HEAD_DIM
EVEN_OUT = HG_HEADS * HG_DV + N_HEADS * HEAD_DIM
D_RNN = D_MODEL
RG_BLOCKS = 4
RG_BW = D_RNN // RG_BLOCKS
CONV_W = 4
RG_C = 8.0
PEER_HEADS = 8
PEER_NK = 128
PEER_EXPERTS = PEER_NK * PEER_NK
PEER_DK = 256
PEER_TOPK = 16
PEER_BLOCK = 128

kernel_name = 'hybrid_diffusion_prefix_step'

def _rmsnorm(x, g):
    x32 = x.astype(jnp.float32)
    y = x32 * lax.rsqrt(jnp.mean(x32 * x32, axis=-1, keepdims=True) + EPS)
    return (y * g.astype(jnp.float32)).astype(x.dtype)

def _axial_rope(x):
    L = x.shape[1]
    n_rows = L // GRID_W
    rows = jnp.repeat(jnp.arange(n_rows), GRID_W)
    cols = jnp.tile(jnp.arange(GRID_W), n_rows)
    half = HEAD_DIM // 2
    nf = half // 2
    inv = 1.0 / (ROPE_BASE ** (jnp.arange(nf, dtype=jnp.float32) / nf))

    def rot(xa, pos):
        ang = pos.astype(jnp.float32)[:, None] * inv[None, :]
        cos = jnp.cos(ang)[None, :, None, :]
        sin = jnp.sin(ang)[None, :, None, :]
        x1, x2 = xa[..., :nf], xa[..., nf:]
        return jnp.concatenate([x1 * cos - x2 * sin, x2 * cos + x1 * sin], axis=-1)

    x32 = x.astype(jnp.float32)
    out = jnp.concatenate([rot(x32[..., :half], rows), rot(x32[..., half:], cols)], axis=-1)
    return out.astype(x.dtype)

def _sink_attention(q, ck, cv, sink, k=None, v=None):
    B, Lq = q.shape[0], q.shape[1]
    scale = HEAD_DIM ** -0.5
    sink_logit = jnp.broadcast_to(
        sink.astype(jnp.float32).reshape(1, KV_HEADS, Q_PER_KV, 1, 1),
        (B, KV_HEADS, Q_PER_KV, ATT_BLOCK, 1))
    windowed = k is not None
    n_ctx = ck.shape[1]
    if windowed:
        pad = ((0, 0), (ATT_BLOCK, ATT_BLOCK), (0, 0), (0, 0))
        kp = jnp.pad(k, pad)
        vp = jnp.pad(v, pad)

    def block(j):
        start = j * ATT_BLOCK
        qb = lax.dynamic_slice_in_dim(q, start, ATT_BLOCK, axis=1)
        logits = [jnp.einsum('bqkgd,bskd->bkgqs', qb, ck).astype(jnp.float32) * scale]
        if windowed:
            kb = lax.dynamic_slice_in_dim(kp, start, 3 * ATT_BLOCK, axis=1)
            vb = lax.dynamic_slice_in_dim(vp, start, 3 * ATT_BLOCK, axis=1)
            qpos = start + jnp.arange(ATT_BLOCK)
            kpos = start - ATT_BLOCK + jnp.arange(3 * ATT_BLOCK)
            ok = ((jnp.abs(qpos[:, None] - kpos[None, :]) <= WINDOW)
                  & (kpos[None, :] >= 0) & (kpos[None, :] < Lq))
            s_loc = jnp.einsum('bqkgd,bskd->bkgqs', qb, kb).astype(jnp.float32) * scale
            logits.append(jnp.where(ok, s_loc, NEG_INF))
        probs = jax.nn.softmax(jnp.concatenate(logits + [sink_logit], axis=-1), axis=-1)
        out = jnp.einsum('bkgqs,bskd->bqkgd', probs[..., :n_ctx].astype(cv.dtype), cv)
        if windowed:
            p_loc = probs[..., n_ctx:n_ctx + 3 * ATT_BLOCK].astype(vb.dtype)
            out = out + jnp.einsum('bkgqs,bskd->bqkgd', p_loc, vb)
        return out

    o = lax.map(block, jnp.arange(Lq // ATT_BLOCK))
    return jnp.moveaxis(o, 0, 1).reshape(B, Lq, N_HEADS * HEAD_DIM)

def _hgrn2_scan(q, k, v, logf, s0):
    B, L, H, DK = q.shape
    DV = v.shape[-1]
    n = L // HG_CHUNK
    mask = jnp.tril(jnp.ones((HG_CHUNK, HG_CHUNK), dtype=bool))

    def chunks(a):
        return a.reshape(B, n, HG_CHUNK, H, a.shape[-1]).swapaxes(0, 1)

    def step(S, inp):
        qc, kc, vc, gc = inp
        b = jnp.cumsum(gc, axis=1)
        bm = b[:, HG_CHUNK // 2 - 1][:, None]
        qi = qc * jnp.exp(b - bm)
        ki = kc * jnp.exp(bm - b)
        A = jnp.where(mask, jnp.einsum('bthd,bshd->bhts', qi, ki), 0.0)
        o = (jnp.einsum('bhts,bshv->bthv', A, vc)
             + jnp.einsum('bthd,bhdv->bthv', qc * jnp.exp(b), S))
        bl = b[:, -1:]
        S = (jnp.exp(bl[:, 0])[..., None] * S
             + jnp.einsum('bshd,bshv->bhdv', kc * jnp.exp(bl - b), vc))
        return S, o

    S, o = lax.scan(step, s0.astype(jnp.float32), (chunks(q), chunks(k), chunks(v), chunks(logf)))
    return o.swapaxes(0, 1).reshape(B, L, H, DV), S

def _even_mixer(h, w_in, w_out, lb_f, lb_b, gn_g, sink, s0f, s0b, ck=None, cv=None):
    B, L, _ = h.shape
    f32 = jnp.float32
    hk = HG_HEADS * HG_DK
    hv = HG_HEADS * HG_DV
    splits = np.cumsum([hk, hk, hk, hv, hv, N_HEADS * HEAD_DIM, KV_HEADS * HEAD_DIM]).tolist()
    zq, zf, zb, zi, zg, aq, ak, av = jnp.split(h @ w_in, splits, axis=-1)
    q = jax.nn.silu(zq.astype(f32)).reshape(B, L, HG_HEADS, HG_DK)
    vi = zi.astype(f32).reshape(B, L, HG_HEADS, HG_DV)

    def gates(z, lb):
        z = z.astype(f32).reshape(B, L, HG_HEADS, HG_DK)
        lb = lb.reshape(HG_HEADS, HG_DK)
        return jnp.log(lb + (1.0 - lb) * jax.nn.sigmoid(z)), (1.0 - lb) * jax.nn.sigmoid(-z)

    gf, kf = gates(zf, lb_f)
    gb, kb = gates(zb, lb_b)

    def flip(a):
        return jnp.flip(a, axis=1)

    o_f, sf = _hgrn2_scan(q, kf, vi, gf, s0f)
    o_b, sb = _hgrn2_scan(flip(q), flip(kb), flip(vi), flip(gb), s0b)
    o = o_f + flip(o_b)
    o = (o * lax.rsqrt(jnp.mean(o * o, axis=-1, keepdims=True) + EPS)).reshape(B, L, hv)
    o_hg = o * gn_g.astype(f32) * jax.nn.silu(zg.astype(f32))
    aq = aq.reshape(B, L, N_HEADS, HEAD_DIM)
    ak = ak.reshape(B, L, KV_HEADS, HEAD_DIM)
    av = av.reshape(B, L, KV_HEADS, HEAD_DIM)
    if ck is None:
        o_att = _sink_attention(aq.reshape(B, L, KV_HEADS, Q_PER_KV, HEAD_DIM), ak, av, sink)
    else:
        qr = _axial_rope(aq).reshape(B, L, KV_HEADS, Q_PER_KV, HEAD_DIM)
        o_att = _sink_attention(qr, ck, cv, sink, _axial_rope(ak), av)
    y = jnp.concatenate([o_hg.astype(h.dtype), o_att.astype(h.dtype)], axis=-1) @ w_out
    return y, ak, av, sf, sb

def _centred_dwconv(x, w, b):
    y = lax.conv_general_dilated(
        x, w[:, None, :].astype(x.dtype), window_strides=(1,),
        padding=[(CONV_W // 2, CONV_W - 1 - CONV_W // 2)],
        dimension_numbers=('NWC', 'WIO', 'NWC'), feature_group_count=x.shape[-1])
    return y + b

def _rglru(x, w_a, b_a, w_x, b_x, lam, h0):
    B, L, D = x.shape
    f32 = jnp.float32
    xb = x.reshape(B, L, RG_BLOCKS, RG_BW)
    r = jax.nn.sigmoid(jnp.einsum('blnc,ncd->blnd', xb, w_a.astype(f32)).reshape(B, L, D) + b_a.astype(f32))
    i = jax.nn.sigmoid(jnp.einsum('blnc,ncd->blnd', xb, w_x.astype(f32)).reshape(B, L, D) + b_x.astype(f32))
    log_a = -RG_C * jax.nn.softplus(-lam.astype(f32)) * r
    a = jnp.exp(log_a)
    u = jnp.sqrt(-jnp.expm1(2.0 * log_a)) * (i * x)
    u = u.at[:, 0].add(a[:, 0] * h0.astype(f32))

    def comb(lhs, rhs):
        a1, b1 = lhs
        a2, b2 = rhs
        return a1 * a2, a2 * b1 + b2

    _, hs = lax.associative_scan(comb, (a, u), axis=1)
    return hs, hs[:, -1]

def _odd_mixer(h, w_in, w_out, cw, cb, w_a, b_a, w_x, b_x, lam, h0f, h0b):
    gate, xr = jnp.split(h @ w_in, 2, axis=-1)
    xc = _centred_dwconv(xr, cw, cb).astype(jnp.float32)
    hf, sf = _rglru(xc, w_a[0], b_a[0], w_x[0], b_x[0], lam[0], h0f)
    hb, sb = _rglru(jnp.flip(xc, axis=1), w_a[1], b_a[1], w_x[1], b_x[1], lam[1], h0b)
    y = (hf + jnp.flip(hb, axis=1)) * jax.nn.gelu(gate.astype(jnp.float32))
    return y.astype(h.dtype) @ w_out, sf, sb

def _peer(h, w_q, keys, u, v):
    B, L, D = h.shape
    xt = h.reshape(B * L // PEER_BLOCK, PEER_BLOCK, D)

    def blk(xb):
        q = (xb @ w_q).reshape(PEER_BLOCK, PEER_HEADS, 2, PEER_DK // 2)
        s1 = jnp.einsum('thd,hnd->thn', q[:, :, 0], keys[0]).astype(jnp.float32)
        s2 = jnp.einsum('thd,hnd->thn', q[:, :, 1], keys[1]).astype(jnp.float32)
        v1, i1 = lax.top_k(s1, PEER_TOPK)
        v2, i2 = lax.top_k(s2, PEER_TOPK)
        cand = (v1[..., :, None] + v2[..., None, :]).reshape(PEER_BLOCK, PEER_HEADS, PEER_TOPK * PEER_TOPK)
        cidx = (i1[..., :, None] * PEER_NK + i2[..., None, :]).reshape(PEER_BLOCK, PEER_HEADS, PEER_TOPK * PEER_TOPK)
        sc, pos = lax.top_k(cand, PEER_TOPK)
        eidx = jnp.take_along_axis(cidx, pos, axis=-1)
        g = jax.nn.softmax(sc, axis=-1)
        act = jax.nn.gelu(jnp.einsum('thkd,td->thk', u[eidx], xb).astype(jnp.float32))
        return jnp.einsum('thk,thkd->td', (g * act).astype(v.dtype), v[eidx])

    return lax.map(blk, xt).reshape(B, L, D)

def _trunk(x, cond, p, ctx):
    B = x.shape[0]
    f32 = jnp.float32
    lbf_all = jnp.cumsum(jax.nn.softmax(p['hgrn_lb_fwd'].astype(f32), axis=0), axis=0)
    lbb_all = jnp.cumsum(jax.nn.softmax(p['hgrn_lb_bwd'].astype(f32), axis=0), axis=0)
    new = {'k': [], 'v': [], 'hf': [], 'hb': [], 'lf': [], 'lb': []}
    for l in range(DEPTH):
        j = l // 2
        mod = (jax.nn.silu(cond) @ p['w_mod'][l] + p['b_mod'][l])[:, None, :]
        sh1, sc1, g1, sh2, sc2, g2 = jnp.split(mod, 6, axis=-1)
        h = _rmsnorm(x, p['norm1_g'][l]) * (1 + sc1) + sh1
        if l % 2 == 0:
            if ctx is None:
                s0f = jnp.zeros((B, HG_HEADS, HG_DK, HG_DV), f32)
                s0b = jnp.zeros((B, HG_HEADS, HG_DK, HG_DV), f32)
                ck = None
                cv = None
            else:
                s0f = ctx['hf'][:, j]
                s0b = ctx['hb'][:, j]
                ck = ctx['k'][:, j]
                cv = ctx['v'][:, j]
            y, kk, vv, sf, sb = _even_mixer(
                h, p['w_in_even'][j], p['w_out_even'][j], lbf_all[j], lbb_all[j],
                p['hgrn_gnorm_g'][j], p['attn_sink'][j], s0f, s0b, ck, cv)
            if ctx is None:
                new['k'].append(kk)
                new['v'].append(vv)
                new['hf'].append(sf)
                new['hb'].append(sb)
        else:
            if ctx is None:
                h0f = jnp.zeros((B, D_RNN), f32)
                h0b = jnp.zeros((B, D_RNN), f32)
            else:
                h0f = ctx['lf'][:, j]
                h0b = ctx['lb'][:, j]
            y, sf, sb = _odd_mixer(
                h, p['w_in_odd'][j], p['w_out_odd'][j], p['conv_w'][j], p['conv_b'][j],
                p['rg_w_a'][j], p['rg_b_a'][j], p['rg_w_x'][j], p['rg_b_x'][j],
                p['rg_lambda'][j], h0f, h0b)
            if ctx is None:
                new['lf'].append(sf)
                new['lb'].append(sb)
        x = x + g1 * y
        h = _rmsnorm(x, p['norm2_g'][l]) * (1 + sc2) + sh2
        x = x + g2 * _peer(h, p['peer_w_q'][l], p['peer_keys'][l], p['peer_u'][l], p['peer_v'][l])
    return _rmsnorm(x, p['final_g']), new

def setup_inputs(seed: int = 0) -> dict:
    key = jax.random.key(seed)
    keys = jax.random.split(key, 48)
    counter = iter(range(48))
    f32 = jnp.float32

    def nk():
        return keys[next(counter)]

    def nrm(shape, scale):
        return scale * jax.random.normal(nk(), shape, f32)

    def gain(shape):
        return 1.0 + 0.05 * jax.random.normal(nk(), shape, f32)

    ua = jax.random.uniform(nk(), (N_ODD, 2, D_RNN), f32, 0.9, 0.999)
    s = ua ** (1.0 / RG_C)
    lam = jnp.log(s) - jnp.log1p(-s)
    D = D_MODEL
    return {
        'x_prompt': nrm((BATCH, SEQ, D), 1.0),
        'x_sample': nrm((DEC_BATCH, DEC_SEQ, D), 1.0),
        'cache_k': nrm((DEC_BATCH, N_EVEN, PAST_LEN, KV_HEADS, HEAD_DIM), 1.0),
        'cache_v': nrm((DEC_BATCH, N_EVEN, PAST_LEN, KV_HEADS, HEAD_DIM), 1.0),
        'state_hgrn_fwd': nrm((DEC_BATCH, N_EVEN, HG_HEADS, HG_DK, HG_DV), 0.5),
        'state_hgrn_bwd': nrm((DEC_BATCH, N_EVEN, HG_HEADS, HG_DK, HG_DV), 0.5),
        'state_lru_fwd': nrm((DEC_BATCH, N_ODD, D_RNN), 0.5),
        'state_lru_bwd': nrm((DEC_BATCH, N_ODD, D_RNN), 0.5),
        'c': nrm((DEC_BATCH, D), 1.0),
        'c_ctx': nrm((D,), 1.0),
        'norm1_g': gain((DEPTH, D)),
        'norm2_g': gain((DEPTH, D)),
        'w_mod': nrm((DEPTH, D, 6 * D), 0.5 * D ** -0.5),
        'b_mod': nrm((DEPTH, 6 * D), 0.02),
        'w_in_even': nrm((N_EVEN, D, EVEN_IN), D ** -0.5),
        'w_out_even': nrm((N_EVEN, EVEN_OUT, D), EVEN_OUT ** -0.5),
        'hgrn_lb_fwd': nrm((N_EVEN + 1, HG_HEADS * HG_DK), 0.1),
        'hgrn_lb_bwd': nrm((N_EVEN + 1, HG_HEADS * HG_DK), 0.1),
        'hgrn_gnorm_g': gain((N_EVEN, HG_HEADS * HG_DV)),
        'attn_sink': nrm((N_EVEN, N_HEADS), 0.5),
        'w_in_odd': nrm((N_ODD, D, 2 * D_RNN), D ** -0.5),
        'w_out_odd': nrm((N_ODD, D_RNN, D), D_RNN ** -0.5),
        'conv_w': nrm((N_ODD, CONV_W, D_RNN), CONV_W ** -0.5),
        'conv_b': nrm((N_ODD, D_RNN), 0.02),
        'rg_w_a': nrm((N_ODD, 2, RG_BLOCKS, RG_BW, RG_BW), RG_BW ** -0.5),
        'rg_b_a': nrm((N_ODD, 2, D_RNN), 0.02),
        'rg_w_x': nrm((N_ODD, 2, RG_BLOCKS, RG_BW, RG_BW), RG_BW ** -0.5),
        'rg_b_x': nrm((N_ODD, 2, D_RNN), 0.02),
        'rg_lambda': lam,
        'peer_w_q': nrm((DEPTH, D, PEER_HEADS * PEER_DK), D ** -0.5),
        'peer_keys': nrm((DEPTH, 2, PEER_HEADS, PEER_NK, PEER_DK // 2), (PEER_DK // 2) ** -0.5),
        'peer_u': nrm((DEPTH, PEER_EXPERTS, D), D ** -0.5),
        'peer_v': nrm((DEPTH, PEER_EXPERTS, D), 1.0),
        'final_g': gain((D,)),
    }

def reference(x_prompt, x_sample, cache_k, cache_v, state_hgrn_fwd, state_hgrn_bwd,
              state_lru_fwd, state_lru_bwd, c, c_ctx, norm1_g, norm2_g, w_mod, b_mod,
              w_in_even, w_out_even, hgrn_lb_fwd, hgrn_lb_bwd, hgrn_gnorm_g, attn_sink,
              w_in_odd, w_out_odd, conv_w, conv_b, rg_w_a, rg_b_a, rg_w_x, rg_b_x, rg_lambda,
              peer_w_q, peer_keys, peer_u, peer_v, final_g):
    params = dict(
        norm1_g=norm1_g, norm2_g=norm2_g, w_mod=w_mod, b_mod=b_mod,
        w_in_even=w_in_even, w_out_even=w_out_even, hgrn_lb_fwd=hgrn_lb_fwd,
        hgrn_lb_bwd=hgrn_lb_bwd, hgrn_gnorm_g=hgrn_gnorm_g, attn_sink=attn_sink,
        w_in_odd=w_in_odd, w_out_odd=w_out_odd, conv_w=conv_w, conv_b=conv_b,
        rg_w_a=rg_w_a, rg_b_a=rg_b_a, rg_w_x=rg_w_x, rg_b_x=rg_b_x, rg_lambda=rg_lambda,
        peer_w_q=peer_w_q, peer_keys=peer_keys, peer_u=peer_u, peer_v=peer_v, final_g=final_g)
    y_prompt, st = _trunk(x_prompt, c_ctx[None, :], params, None)
    cache = dict(k=cache_k, v=cache_v, hf=state_hgrn_fwd, hb=state_hgrn_bwd,
                 lf=state_lru_fwd, lb=state_lru_bwd)
    y_sample, _ = _trunk(x_sample, c, params, cache)
    new_k = jnp.stack(st['k'], axis=1)
    new_v = jnp.stack(st['v'], axis=1)
    new_hgrn_fwd = jnp.stack(st['hf'], axis=1)
    new_hgrn_bwd = jnp.stack(st['hb'], axis=1)
    new_lru_fwd = jnp.stack(st['lf'], axis=1)
    new_lru_bwd = jnp.stack(st['lb'], axis=1)
    return (y_prompt, y_sample, new_k, new_v, new_hgrn_fwd, new_hgrn_bwd, new_lru_fwd, new_lru_bwd)


_drawn_inputs = setup_inputs


def setup_inputs(seed=0):
    import zlib

    import numpy as np

    out = dict(_drawn_inputs(seed))
    spreads = {}
    factors = {'state_hgrn_fwd': 131.923,
     'state_hgrn_bwd': 110.381,
     'attn_sink': 8.0,
     'rg_b_a': 8.0,
     'rg_b_x': 6.266}
    for name, (base, spread) in spreads.items():
        noise = np.random.default_rng([zlib.crc32(name.encode()), seed]).standard_normal(out[name].shape)
        drawn = base * np.exp(spread * noise) if base else spread * noise
        out[name] = __import__('jax').numpy.asarray(drawn.astype(out[name].dtype))
    for name, factor in factors.items():
        out[name] = (out[name] * factor).astype(out[name].dtype)
    return out
```

```python
from contextlib import ExitStack

import numpy as np

import concourse.bass as bass
from concourse import mybir

F32 = mybir.dt.float32
U32 = mybir.dt.uint32
ALU = mybir.AluOpType
ACT = mybir.ActivationFunctionType
AX = mybir.AxisListType

PHASES = ("mod", "even", "peer0", "odd", "peer1")

P = 128
D = 1024
KD = D // P
LP, LS = 128, 512
T = LP + LS
NB = T // P
SB = LS // P
EPS = 1e-6
NEG = -1e30
LAYERS = 2
HEADS, NK, TOPK, EXPERTS = 8, 128, 16, 16384
SLOTS = 10
NDIAG = 4
PER_HEAD = NB * TOPK
GROUP = 2
HG, CH = 4, 64
NCH = T // CH
SCH = LS // CH
NG, HD = 4, 64
SCALE = HD ** -0.5
RB = 4


def cond_of(b):
    return 0 if b < SB else 1


def wait_apart(eng, sem, value):
    eng.wait_ge(sem, value)
    eng.nop(nofuse=True)


class Count:

    def __init__(self, eng, sem, base=0, apart=False):
        self.eng, self.sem, self.base, self.n, self.apart = eng, sem, base, 0, apart

    def add(self, ins):
        ins.then_inc(self.sem, 1)
        self.n += 1

    def wait(self):
        self.eng.wait_ge(self.sem, self.base + self.n)
        if self.apart:
            self.eng.nop(nofuse=True)


def broadcast_rows(ap, lo, n):
    return ap[lo:lo + n].unsqueeze(0).broadcast_to([P, n])


def phase(nc, name, body):
    with ExitStack() as ctx:
        def sb(what, shape, dt=F32):
            return ctx.enter_context(nc.sbuf_tensor(f"{name}_{what}", shape, dt))

        def ps(what, cols):
            return ctx.enter_context(nc.psum_tensor(f"{name}_{what}", [P, cols], F32))

        used = []

        def sem(what):
            used.append(ctx.enter_context(nc.semaphore(f"{name}_{what}")))
            return used[-1]

        body(sb, ps, sem)

        with nc.Block() as block:
            @block.gpsimd
            def _(pool):
                numbers = sorted(one.num for one in used)
                start = numbers[0]
                for n, after in zip(numbers, numbers[1:] + [None]):
                    if after != n + 1:
                        pool.sem_clear(range(start, n + 1))
                        start = after


def norm_parts(sb, sem, pre, X, H, HT, ident, AB, ab_landed, ab_target, junk, tp):
    ss = sb(pre + "ss", [P, NB])
    rt = sb(pre + "rt", [P, NB])
    rs = sb(pre + "rs", [P, NB])
    squared, rooted, inverted = sem(pre + "squared"), sem(pre + "rooted"), sem(pre + "inverted")
    scaled, ready = sem(pre + "scaled"), sem(pre + "h_ready")
    turned, stored = sem(pre + "turned"), sem(pre + "stored")

    def act(eng, x_ready=None):
        if x_ready:
            eng.wait_ge(*x_ready)
        for b in range(NB):
            if b:
                eng.wait_ge(squared, b)
            eng.activation(junk, X[:, b, :], ACT.Square, accum_out=ss[:, b:b + 1]).then_inc(squared, 1)
        eng.wait_ge(squared, NB)
        eng.activation(rt[:, :], ss[:, :], ACT.Copy, scale=1.0 / D, bias=EPS).then_inc(rooted, 1)
        eng.wait_ge(rooted, 1)
        eng.activation(rt[:, :], rt[:, :], ACT.Sqrt).then_inc(rooted, 1)
        for b in range(NB):
            eng.wait_ge(turned, b + 1)
            eng.activation(HT[:, :, b * P:(b + 1) * P], tp[b % 2][:, :].rearrange("p (k t) -> p k t", k=KD),
                           ACT.Copy).then_inc(stored, 1)

    def dve(eng):
        eng.wait_ge(rooted, 2)
        eng.reciprocal(rs[:, :], rt[:, :]).then_inc(inverted, 1)
        eng.wait_ge(inverted, 1)
        eng.wait_ge(ab_landed, ab_target)
        for b in range(NB):
            c = cond_of(b)
            eng.scalar_tensor_tensor(out=H[:, b, :], in0=X[:, b, :], scalar=rs[:, b:b + 1],
                                     in1=AB[:, 0, c, :], op0=ALU.mult, op1=ALU.mult).then_inc(scaled, 1)
            eng.wait_ge(scaled, b + 1)
            eng.tensor_tensor(H[:, b, :], H[:, b, :], AB[:, 1, c, :], ALU.add).then_inc(ready, 1)

    def pe(eng):
        for b in range(NB):
            eng.wait_ge(ready, b + 1)
            if b >= 2:
                eng.wait_ge(stored, b - 1)
            for k in range(KD):
                last = eng.transpose(tp[b % 2][:, k * P:(k + 1) * P], H[:, b, k * P:(k + 1) * P], ident[:, :])
            last.then_inc(turned, 1)

    return act, dve, pe, stored, NB


def modulation(nc, X, ident, io):
    NCK = LAYERS * 6 * D // 512

    def body(sb, ps, sem):
        condT = sb("condT", [P, KD, 2])
        sgm = sb("sgm", [P, KD, 2])
        w = sb("wmod", [P, 2, KD * 512])
        bias = sb("bmod", [2, NCK * 512])
        rows = sb("rows", [2, NCK * 512])
        gains = sb("gains", [2, 2, LAYERS, D])
        out = [ps(f"modp{i}", 512) for i in range(2)]
        x_in, cond_in, small_in = sem("x_in"), sem("cond_in"), sem("small_in")
        w_in = [sem(f"wmod_in{i}") for i in range(2)]
        sg_done, silu_done = sem("sg_done"), sem("silu_done")
        chunk_done, chunk_read = sem("chunk_done"), sem("chunk_read")
        gained, rows_out, ident0, ident1 = sem("gained"), sem("rows_out"), sem("ident0"), sem("ident1")

        with nc.Block() as block:
            @block.sync
            def _(sp):
                with sp.Fori(0, NCK // 2) as i:
                    for s in range(2):
                        sp.wait_ge(chunk_done, i * 2 + s + 1)
                        sp.dma_start(w[:, s, :], io["w_mod"][bass.ds(i * 2 + s, 1), :, :].rearrange("a p n -> (a p) n"))\
                          .then_inc(w_in[s], 16)
                sp.wait_ge(gained, 2 * LAYERS)
                sp.dma_start(io["mod_rows"].rearrange("(c n) -> c n", c=2), rows[:, :]).then_inc(rows_out, 16)
                sp.wait_ge(rows_out, 16)

            @block.scalar
            def _(act):
                act.dma_start(condT[:, :, :], io["condT"]).then_inc(cond_in, 16)
                act.dma_start(X[:, 0:SB, :], io["x_sample"].rearrange("o (b p) d -> (o p) b d", p=P)).then_inc(x_in, 16)
                act.dma_start(X[:, SB, :], io["x_prompt"].rearrange("o p d -> (o p) d")).then_inc(x_in, 16)
                act.dma_start(bias[:, :], io["b_mod"].rearrange("l n -> (l n)").unsqueeze(0).broadcast_to([2, NCK * 512])).then_inc(small_in, 16)
                for n, name in enumerate(("norm1_g", "norm2_g")):
                    act.dma_start(gains[:, n, :, :].rearrange("p l d -> p (l d)"),
                                  io[name].rearrange("l d -> (l d)").unsqueeze(0).broadcast_to([2, LAYERS * D])).then_inc(small_in, 16)
                act.wait_ge(cond_in, 16)
                act.activation(sgm[:, :, :], condT[:, :, :], ACT.Sigmoid).then_inc(sg_done, 1)
                act.wait_ge(x_in, 32)

            @block.gpsimd
            def _(pool):
                pool.memset(ident[:, :], 0.0).then_inc(ident0, 1)
                pool.wait_ge(ident0, 1)
                pool.affine_select(out=ident[:, :], in_=ident[:, :], compare_op=ALU.not_equal, fill=1.0,
                                   base=0, pattern=[[-1, P]], channel_multiplier=1).then_inc(ident1, 1)
                pool.wait_ge(ident1, 1)

            @block.vector
            def _(dve):
                dve.sem_inc(chunk_read, 2)
                dve.wait_ge(sg_done, 1)
                dve.tensor_tensor(condT[:, :, :], condT[:, :, :], sgm[:, :, :], ALU.mult).then_inc(silu_done, 1)
                dve.wait_ge(small_in, 48)
                with dve.Fori(0, NCK // 2) as i:
                    for s in range(2):
                        dve.wait_ge(chunk_done, i * 2 + s + 3)
                        dve.tensor_tensor(rows[:, bass.ds(i * 1024 + s * 512, 512)], out[s][0:2, :],
                                          bias[:, bass.ds(i * 1024 + s * 512, 512)], ALU.add).then_inc(chunk_read, 1)
                dve.wait_ge(chunk_read, NCK + 2)
                for layer in range(LAYERS):
                    for n in range(2):
                        lo = layer * 6 * D + (3 * n + 1) * D
                        dve.scalar_tensor_tensor(out=rows[:, lo:lo + D], in0=rows[:, lo:lo + D], scalar=1.0,
                                                 in1=gains[:, n, layer, :], op0=ALU.add, op1=ALU.mult).then_inc(gained, 1)

            @block.tensor
            def _(pe):
                pe.sem_inc(chunk_done, 2)
                pe.wait_ge(silu_done, 1)
                with pe.Fori(0, NCK // 2) as i:
                    for s in range(2):
                        pe.wait_ge(w_in[s], i * 16 + 16)
                        pe.wait_ge(chunk_read, i * 2 + s + 1)
                        for k in range(KD):
                            last = pe.matmul(out[s][0:2, :], condT[:, k, :], w[:, s, k * 512:(k + 1) * 512],
                                             start=(k == 0), stop=(k == KD - 1))
                        last.then_inc(chunk_done, 1)

    phase(nc, "mod", body)


def load_mod(eng, io, dst, layer, section, landed):
    for c in range(2):
        lo = c * LAYERS * 6 * D + layer * 6 * D + section * D
        eng.dma_start(dst[:, c, :], broadcast_rows(io["mod_rows"], lo, D)).then_inc(landed, 16)


def project_and_peer(nc, X, H, HT, ident, iota16, layer, io):
    def body(sb, ps, sem):
        pre = f"p{layer}_"
        G2 = sb("G2", [P, 2, D])
        ring = sb("ring", [P, SLOTS, 2 * D])
        AB = ring[:, 0:2, :].rearrange("p s (c d) -> p s c d", c=2)
        G1 = ring[:, 2, :].rearrange("p (c d) -> p c d", c=2)
        squares = ring[:, 3, 0:D]
        w_out = ring[:, 4:8, :].rearrange("p s (k n) -> p (s k) n", n=D)
        ss, rt, rs = sb("ss", [P, NB]), sb("rt", [P, NB]), sb("rs", [P, NB])
        wq = sb("wq", [P, KD, 2 * P])
        keys = sb("keys", [P, 2, P])
        qT = sb("qT", [P, 2, T])
        qN = sb("qN", [P, 2, T])
        best = sb("best", [P, 2, TOPK])
        besti = sb("besti", [P, 2, TOPK], U32)
        bestf = sb("bestf", [P, 2, TOPK])
        work = sb("work", [P, 2, NK])
        cand = sb("cand", [P, TOPK * TOPK])
        candw = sb("candw", [P, TOPK * TOPK])
        top = sb("top", [P, TOPK])
        negtop = sb("negtop", [P, 1])
        topi = sb("topi", [P, TOPK], U32)
        pab = sb("pab", [P, 2, TOPK], U32)
        onehot = sb("onehot", [P, 2, TOPK, TOPK])
        pick = sb("pick", [P, 2, TOPK])
        index = sb("index", [P, PER_HEAD], U32)
        expo = sb("expo", [P, TOPK])
        total = sb("total", [P, 1])
        inv = sb("inv", [P, 1])
        gate = sb("gate", [P, PER_HEAD])
        dots = sb("dots", [P, PER_HEAD])
        acts = sb("acts", [P, PER_HEAD])
        diag = sb("diag", [P, NDIAG, P])
        tmp = sb("tmp", [P, D])
        acc = [ps(f"acc{i}", 1024) for i in range(2)]
        qp = ps("qp", 1024)
        sc = ps("sc", 512)
        q0 = ps("q0", 512)

        mod_in, g2_in = sem(pre + "mod_in"), sem(pre + "g2_in")
        w_in = [sem(pre + f"w_in{i}") for i in range(KD // 2)]
        g1_in, projected, gated, x_ready = (sem(pre + n) for n in ("g1_in", "projected", "gated", "x_ready"))
        squared, shifted, rooted, inverted = (sem(pre + n) for n in ("squared", "shifted", "rooted", "inverted"))
        scaled, h_ready, turned, h_stored = (sem(pre + n) for n in ("scaled", "h_ready", "turned", "h_stored"))
        q0_done, q0_stored = sem(pre + "q0_done"), sem(pre + "q0_stored")
        landed = [sem(pre + f"landed{i}") for i in range(SLOTS)]
        slot_free = sem(pre + "slot_free")
        index_ready = sem(pre + "index_ready")
        dot_done, act_done, diag_done = sem(pre + "dot_done"), sem(pre + "act_done"), sem(pre + "diag_done")
        added = sem(pre + "added")
        wq_in, keys_in = sem(pre + "wq_in"), sem(pre + "keys_in")
        q_done, q_stored, qt_ready = sem(pre + "q_done"), sem(pre + "q_stored"), sem(pre + "qt_ready")
        sc_done, sc_used = sem(pre + "sc_done"), sem(pre + "sc_used")
        top_ready, exp_done, rstep = sem(pre + "top_ready"), sem(pre + "exp_done"), sem(pre + "rstep")
        tmp_done = sem(pre + "tmp_done")
        RSTEPS = 26
        w_q, kT, uv = io["w_q"], io["keysT"], io["uv"]

        def heads(eng, body_of_head):
            with eng.Fori(0, HEADS - 1) as h:
                body_of_head(h, False)
            body_of_head(HEADS - 1, True)

        def next_unit(b, last):
            return None if last and b == NB - 1 else (b + 1) % NB

        with nc.Block() as block:
            @block.sync
            def _(sp):
                for i in range(KD // 2):
                    sp.dma_start(w_out[:, 2 * i:2 * i + 2, :],
                                 io["w_out"][layer, 2 * i * P:(2 * i + 2) * P, :].rearrange("(k p) n -> p k n", p=P))\
                        .then_inc(w_in[i], 16)
                load_mod(sp, io, G1, layer, 2, g1_in)
                load_mod(sp, io, AB[:, 0, :, :], layer, 4, mod_in)
                load_mod(sp, io, AB[:, 1, :, :], layer, 3, mod_in)
                sp.dma_start(wq[:, :, :].rearrange("p k n -> p (k n)"), w_q[layer * HEADS, :, :]).then_inc(wq_in, 16)
                sp.dma_start(keys[:, :, :].rearrange("p a n -> p (a n)"), kT[layer * HEADS, :, :]).then_inc(keys_in, 16)
                load_mod(sp, io, G2, layer, 5, g2_in)
                with sp.Fori(0, HEADS - 1) as h:
                    sp.wait_ge(q_done, h * 2 + 2)
                    sp.dma_start(wq[:, :, :].rearrange("p k n -> p (k n)"),
                                 w_q[bass.ds(h + (layer * HEADS + 1), 1), :, :].rearrange("a p n -> (a p) n")).then_inc(wq_in, 16)
                    sp.wait_ge(sc_done, h * NB + NB)
                    sp.dma_start(keys[:, :, :].rearrange("p a n -> p (a n)"),
                                 kT[bass.ds(h + (layer * HEADS + 1), 1), :, :].rearrange("a p n -> (a p) n")).then_inc(keys_in, 16)
                sp.wait_ge(g2_in, 32)

            @block.gpsimd
            def _(pool):
                pool.wait_ge(h_ready, NB)

                def head(h, last):
                    for j in range(PER_HEAD):
                        if j % TOPK == 0:
                            pool.wait_ge(index_ready, h * NB + (j // TOPK + 1))
                        wait_apart(pool, slot_free, h * PER_HEAD + (j + 1))
                        pool.indirect_dma_start(ring[:, j % SLOTS, :], None, uv[:, :],
                                                bass.IndirectOffsetOnAxis(ap=index[:, j:j + 1], axis=0),
                                                element_offset=layer * EXPERTS * 2 * D)\
                            .then_inc(landed[j % SLOTS], 16)

                heads(pool, head)

            @block.scalar
            def _(act):
                def store_turned(b):
                    act.wait_ge(turned, b + 1)
                    act.activation(HT[:, :, b * P:(b + 1) * P], qp[:, :].rearrange("p (k t) -> p k t", k=KD),
                                   ACT.Copy).then_inc(h_stored, 1)

                def store_q0(b):
                    act.wait_ge(q0_done, b + 1)
                    act.activation(qT[:, :, b * P:(b + 1) * P], q0[:, 0:2 * P].rearrange("p (a t) -> p a t", a=2),
                                   ACT.Copy).then_inc(q0_stored, 1)

                for b in range(NB):
                    act.wait_ge(x_ready, b + 1)
                    act.activation(squares, X[:, b, :], ACT.Square, accum_out=ss[:, b:b + 1]).then_inc(squared, 1)
                    act.wait_ge(squared, b + 1)
                    act.activation(rt[:, b:b + 1], ss[:, b:b + 1], ACT.Copy, scale=1.0 / D, bias=EPS).then_inc(shifted, 1)
                    act.wait_ge(shifted, b + 1)
                    act.activation(rt[:, b:b + 1], rt[:, b:b + 1], ACT.Sqrt).then_inc(rooted, 1)
                    if b >= 1:
                        store_turned(b - 1)
                    if b >= 2:
                        store_q0(b - 2)
                store_turned(NB - 1)
                store_q0(NB - 2)
                store_q0(NB - 1)
                act.wait_ge(q0_stored, NB)
                act.sem_inc(q_stored, 2)
                act.sem_inc(qt_ready, 1)

                def exponent(unit):
                    act.wait_ge(top_ready, unit + 1)
                    act.activation(expo[:, :], top[:, :], ACT.Exp, bias=negtop[:, 0:1],
                                   accum_out=total[:, 0:1]).then_inc(exp_done, 1)

                def store_q(h, half):
                    act.wait_ge(q_done, h * 2 + (half + 1))
                    act.activation(qN[:, half, :], qp[:, 0:T], ACT.Copy).then_inc(q_stored, 1)

                def hand_q(h):
                    act.wait_ge(q_stored, h * 2 + 2)
                    act.activation(qT[:, :, :], qN[:, :, :], ACT.Copy).then_inc(qt_ready, 1)

                exponent(0)

                def head(h, last):
                    for g in range(PER_HEAD // GROUP):
                        b, s = divmod(g, TOPK // GROUP)
                        act.wait_ge(dot_done, h * PER_HEAD + GROUP * (g + 1))
                        act.activation(acts[:, GROUP * g:GROUP * (g + 1)], dots[:, GROUP * g:GROUP * (g + 1)],
                                       ACT.Gelu_apprx_tanh).then_inc(act_done, 1)
                        if s == 2 and next_unit(b, last) is not None:
                            exponent(h * NB + (b + 1))
                        if not last and g == 14:
                            store_q(h + 1, 0)
                        if not last and g == 26:
                            store_q(h + 1, 1)
                        if not last and g == 28:
                            act.wait_ge(sc_done, h * NB + NB)
                            hand_q(h + 1)

                heads(act, head)

            @block.vector
            def _(dve):
                dve.sem_inc(added, 1)

                def residual(b):
                    dve.wait_ge(projected, b + 1)
                    dve.tensor_tensor(tmp[:, :], acc[b % 2][:, :], G1[:, cond_of(b), :], ALU.mult).then_inc(gated, 1)
                    dve.wait_ge(gated, b + 1)
                    dve.tensor_tensor(X[:, b, :], X[:, b, :], tmp[:, :], ALU.add).then_inc(x_ready, 1)

                def norm(b):
                    c = cond_of(b)
                    dve.wait_ge(rooted, b + 1)
                    dve.reciprocal(rs[:, b:b + 1], rt[:, b:b + 1]).then_inc(inverted, 1)
                    dve.wait_ge(inverted, b + 1)
                    dve.scalar_tensor_tensor(out=H[:, b, :], in0=X[:, b, :], scalar=rs[:, b:b + 1],
                                             in1=AB[:, 0, c, :], op0=ALU.mult, op1=ALU.mult).then_inc(scaled, 1)
                    dve.wait_ge(scaled, b + 1)
                    dve.tensor_tensor(H[:, b, :], H[:, b, :], AB[:, 1, c, :], ALU.add).then_inc(h_ready, 1)

                def route_a(unit):
                    r = Count(dve, rstep, unit * RSTEPS, apart=True)
                    halves = [sc[:, 0:NK], sc[:, NK:2 * NK]]
                    wait_apart(dve, sc_done, unit + 1)
                    for a in range(2):
                        r.add(dve.max(best[:, a, 0:8], halves[a]))
                    r.wait()
                    for a in range(2):
                        r.add(dve.match_replace(work[:, a, :], best[:, a, 0:8], halves[a], -3e38))
                    r.wait()
                    for a in range(2):
                        r.add(dve.max(best[:, a, 8:16], work[:, a, :]))
                    for a in range(2):
                        r.add(dve.max_index(besti[:, a, 0:8], best[:, a, 0:8], halves[a]))
                    r.wait()
                    dve.sem_inc(sc_used, 1)
                    return r

                def route_b(r):
                    for a in range(2):
                        r.add(dve.max_index(besti[:, a, 8:16], best[:, a, 8:16], work[:, a, :]))
                    r.add(dve.tensor_tensor(cand[:, :].rearrange("p (a b) -> p a b", a=TOPK),
                                            best[:, 0, :].unsqueeze(2).broadcast_to([P, TOPK, TOPK]),
                                            best[:, 1, :].unsqueeze(1).broadcast_to([P, TOPK, TOPK]), ALU.add))
                    r.wait()
                    r.add(dve.tensor_scalar(bestf[:, 0, :], besti[:, 0, :], float(NK), None, ALU.mult))
                    r.add(dve.tensor_copy(bestf[:, 1, :], besti[:, 1, :]))
                    r.add(dve.max(top[:, 0:8], cand[:, :]))
                    r.wait()
                    r.add(dve.match_replace(candw[:, :], top[:, 0:8], cand[:, :], -3e38))
                    r.add(dve.tensor_scalar(negtop[:, :], top[:, 0:1], -1.0, None, ALU.mult))
                    r.add(dve.max_index(topi[:, 0:8], top[:, 0:8], cand[:, :]))
                    r.wait()

                def route_c(r, b):
                    r.add(dve.max(top[:, 8:16], candw[:, :]))
                    r.wait()
                    dve.sem_inc(top_ready, 1)
                    r.add(dve.max_index(topi[:, 8:16], top[:, 8:16], candw[:, :]))
                    r.wait()
                    r.add(dve.tensor_scalar(pab[:, 0, :], topi[:, :], 4, None, ALU.logical_shift_right))
                    r.add(dve.tensor_scalar(pab[:, 1, :], topi[:, :], TOPK - 1, None, ALU.bitwise_and))
                    r.wait()
                    r.add(dve.tensor_tensor(onehot[:, :, :, :].rearrange("p a k r -> p (a k) r"),
                                            pab[:, :, :].rearrange("p a k -> p (a k)").unsqueeze(2).broadcast_to([P, 2 * TOPK, TOPK]),
                                            iota16[:, :].unsqueeze(1).broadcast_to([P, 2 * TOPK, TOPK]), ALU.is_equal))
                    r.wait()
                    r.add(dve.tensor_tensor(onehot[:, :, :, :], onehot[:, :, :, :],
                                            bestf[:, :, :].unsqueeze(2).broadcast_to([P, 2, TOPK, TOPK]), ALU.mult))
                    r.wait()
                    r.add(dve.tensor_reduce(pick[:, :, :].rearrange("p a k -> p (a k)"),
                                            onehot[:, :, :, :].rearrange("p a k r -> p (a k) r"), AX.X, ALU.add))
                    r.wait()
                    dve.tensor_tensor(index[:, b * TOPK:(b + 1) * TOPK], pick[:, 0, :], pick[:, 1, :],
                                      ALU.add).then_inc(index_ready, 1)

                def route_d(r, unit, b):
                    dve.wait_ge(exp_done, unit + 1)
                    r.add(dve.reciprocal(inv[:, :], total[:, :]))
                    r.wait()
                    r.add(dve.tensor_scalar(gate[:, b * TOPK:(b + 1) * TOPK], expo[:, :], inv[:, 0:1], None, ALU.mult))
                    r.wait()
                    assert r.n == RSTEPS, r.n

                dve.wait_ge(g1_in, 32)
                dve.wait_ge(mod_in, 64)
                for b in range(NB):
                    residual(b)
                    norm(b)
                    if b == 2:
                        r = route_a(0)
                        route_b(r)
                    if b == 3:
                        route_c(r, 0)
                route_d(r, 0, 0)
                dve.wait_ge(g2_in, 32)

                def dot(h, j):
                    dve.wait_ge(landed[j % SLOTS], (h * (PER_HEAD // SLOTS) + (j // SLOTS + 1)) * 16)
                    u = ring[:, j % SLOTS, 0:D]
                    dve.tensor_tensor_reduce(u, u, H[:, j // TOPK, :], 1.0, 0.0, ALU.mult, ALU.add,
                                             dots[:, j:j + 1]).then_inc(dot_done, 1)

                def weight(h, g):
                    dve.wait_ge(act_done, h * (PER_HEAD // GROUP) + (g + 1))
                    for j in range(GROUP * g, GROUP * (g + 1)):
                        dve.wait_ge(slot_free, h * PER_HEAD + (j + 1 + SLOTS - NDIAG))
                        dve.tensor_scalar(diag[:, j % NDIAG, :], ident[:, :], acts[:, j:j + 1], gate[:, j:j + 1],
                                          ALU.mult, ALU.mult).then_inc(diag_done, 1)

                def add_unit(h, b):
                    dve.wait_ge(slot_free, h * PER_HEAD + ((b + 1) * TOPK + SLOTS))
                    dve.tensor_tensor(tmp[:, :], acc[b % 2][:, :], G2[:, cond_of(b), :], ALU.mult).then_inc(tmp_done, 1)
                    dve.wait_ge(tmp_done, h * NB + (b + 1))
                    dve.tensor_tensor(X[:, b, :], X[:, b, :], tmp[:, :], ALU.add).then_inc(added, 1)

                def head(h, last):
                    r = None
                    for g in range(PER_HEAD // GROUP):
                        b, s = divmod(g, TOPK // GROUP)
                        for j in range(GROUP * g, GROUP * (g + 1)):
                            dot(h, j)
                        if g:
                            weight(h, g - 1)
                        nb = next_unit(b, last)
                        unit = h * NB + (b + 1)
                        if nb is not None:
                            if s == 0:
                                r = route_a(unit)
                            if s == 1:
                                route_b(r)
                            if s == 2:
                                route_c(r, nb)
                            if s == 3:
                                route_d(r, unit, nb)
                        if s == 3 and b:
                            add_unit(h, b - 1)
                    weight(h, PER_HEAD // GROUP - 1)
                    add_unit(h, NB - 1)

                heads(dve, head)

            @block.tensor
            def _(pe):
                pe.sem_inc(slot_free, SLOTS)

                def project(b):
                    if b >= 2:
                        pe.wait_ge(gated, b - 1)
                    for k in range(KD):
                        if b == 0 and k % 2 == 0:
                            pe.wait_ge(w_in[k // 2], 16)
                        for lo in (0, 512):
                            last = pe.matmul(acc[b % 2][:, lo:lo + 512], H[:, b, k * P:(k + 1) * P],
                                             w_out[:, k, lo:lo + 512], start=(k == 0), stop=(k == KD - 1))
                    last.then_inc(projected, 1)

                def turn(b):
                    pe.wait_ge(h_ready, b + 1)
                    if b:
                        pe.wait_ge(h_stored, b)
                    for k in range(KD):
                        last = pe.transpose(qp[:, k * P:(k + 1) * P], H[:, b, k * P:(k + 1) * P], ident[:, :])
                    last.then_inc(turned, 1)

                def first_query(b):
                    pe.wait_ge(h_stored, b + 1)
                    if b:
                        pe.wait_ge(q0_stored, b)
                    else:
                        pe.wait_ge(wq_in, 16)
                    for a in range(2):
                        for k in range(KD):
                            last = pe.matmul(q0[:, a * P:(a + 1) * P], wq[:, k, a * P:(a + 1) * P],
                                             HT[:, k, b * P:(b + 1) * P], start=(k == 0), stop=(k == KD - 1))
                    last.then_inc(q0_done, 1)

                def query(h, n):
                    half, k = divmod(n, KD)
                    if n == 0:
                        pe.wait_ge(wq_in, h * 16 + 16)
                    if k == 0:
                        pe.wait_ge(q_stored, h * 2 + half)
                    for lo, hi in ((0, LS), (LS, T)):
                        last = pe.matmul(qp[:, lo:hi], wq[:, k, half * P:(half + 1) * P], HT[:, k, lo:hi],
                                         start=(k == 0), stop=(k == KD - 1), skip_group_check=True)
                    if k == KD - 1:
                        last.then_inc(q_done, 1)

                def scores(h, b, unit):
                    if unit is None:
                        pe.wait_ge(q0_stored, 1)
                        pe.wait_ge(keys_in, 16)
                    else:
                        pe.wait_ge(qt_ready, h + 1)
                        pe.wait_ge(keys_in, h * 16 + 16)
                        pe.wait_ge(sc_used, unit)
                    for a in range(2):
                        last = pe.matmul(sc[:, a * NK:(a + 1) * NK], qT[:, a, b * P:(b + 1) * P], keys[:, a, :],
                                         start=True, stop=True)
                    last.then_inc(sc_done, 1)

                for b in range(NB):
                    project(b)
                    if b >= 1:
                        turn(b - 1)
                    if b >= 2:
                        first_query(b - 2)
                    if b == 2:
                        scores(0, 0, None)
                turn(NB - 1)
                first_query(NB - 2)
                first_query(NB - 1)
                pe.wait_ge(q0_done, NB)
                pe.sem_inc(q_done, 2)

                def head(h, last):
                    for b in range(NB):
                        nb = next_unit(b, last)
                        if nb is not None:
                            scores(h + 1 if nb == 0 else h, nb, h * NB + (b + 1))
                        pe.wait_ge(added, h * NB + (1 if b == 0 else b))
                        for e in range(TOPK):
                            j = b * TOPK + e
                            pe.wait_ge(diag_done, h * PER_HEAD + (j + 1))
                            for lo in (0, 512):
                                last_mm = pe.matmul(acc[b % 2][:, lo:lo + 512], diag[:, j % NDIAG, :],
                                                    ring[:, j % SLOTS, D + lo:D + lo + 512],
                                                    start=(e == 0), stop=(e == TOPK - 1))
                            last_mm.then_inc(slot_free, 1)
                            if not last and j % 3 == 2 and j // 3 < 2 * KD:
                                query(h + 1, j // 3)

                heads(pe, head)

    phase(nc, f"peer{layer}", body)


def hgrn(nc, X, HT, YT, watt, ident, io):
    def body(sb, ps, sem):
        wh = sb("wh", [P, KD, 5 * P])
        lbr = sb("lbr", [P, 2, 2, HG])
        lbx = sb("lbx", [P, 2, HG])
        lbe = sb("lbe", [P, 2, 2, HG])
        lb = sb("lb", [P, 2, HG])
        oml = sb("oml", [P, 2, HG])
        gn = sb("gn", [P, HG])
        reset = sb("reset", [P, T])
        tri = sb("tri", [P, 2, P])
        AB = sb("ABe", [P, 2, 2, D])
        work = lambda n: sb(n, [P, T])
        Q, SQ = work("Q"), work("SQ")
        V = sb("V", [P, NB, P])
        Vm = sb("Vm", [P, NB, 2, P])
        ZG = sb("ZG", [P, NB, P])
        ON = sb("ON", [P, NB, P])
        K = [work("Kf"), work("Kb")]
        G = [work("Gf"), work("Gb")]
        B = [work("Bf"), work("Bb")]
        QI = [work("QIf"), work("QIb")]
        KI = [work("KIf"), work("KIb")]
        QB = [work("QBf"), work("QBb")]
        KL = [work("KLf"), work("KLb")]
        KLT = [work("KLTf"), work("KLTb")]
        AT = [work("ATf"), work("ATb")]
        EBL = sb("EBL", [P, 2, NCH])
        S = [sb("Sf", [P, NCH + 1, P]), sb("Sb", [P, NCH + 1, P])]
        SS = sb("SS", [P, NB])
        RT = sb("RT", [P, NB])
        RS = sb("RS", [P, NB])
        D0, D1, D2, D3 = (ps(f"D{i}", 1024) for i in range(4))

        mod_in, lb_in, gn_in, watt_in = sem("e_mod_in"), sem("lb_in"), sem("gn_in"), sem("watt_in")
        n_act, n_dve, n_pe, h_stored, n_stored = norm_parts(sb, sem, "e_", X, YT, HT, ident, AB, mod_in, 64, D2[:, :], [D0, D1])
        consts, czero = sem("consts"), sem("czero")
        lb_step, lb_exp, lb_ready = sem("lb_step"), sem("lb_exp"), sem("lb_ready")
        wh_in, s0_in, st_out = sem("wh_in"), sem("s0_in"), sem("st_out")
        proj = [sem(f"proj_{n}") for n in "fbqv"]
        sig_done, q_made, ln_done, diff_done, exp_done = (sem(n) for n in ("sig_done", "q_made", "ln_done", "diff_done", "e_exp"))
        v_done, zg_sig, vg_read, vm_done = (sem(n) for n in ("v_done", "zg_sig", "vg_read", "vm_done"))
        kl_done, klt_psum, klt_done = sem("kl_done"), sem("klt_psum"), sem("klt_done")
        at_psum, at_done, u_done, s_done = sem("at_psum"), sem("at_done"), sem("u_done"), sem("s_done")
        o_done, o_sq, ss_done, rt_done = sem("o_done"), sem("o_sq"), sem("ss_done"), sem("rt_done")
        on_done, on_turned, head_done, dstep = sem("on_done"), sem("on_turned"), sem("head_done"), sem("dstep")
        states_done = sem("states_done")
        st_free = sem("st_free")
        DSTEPS = 31
        NCONST = 12
        first = [0, CH - 1]
        final = [CH - 1, 0]
        middle = [CH // 2 - 1, CH // 2]

        def by_chunk(t):
            return t[:, :].rearrange("p (c t) -> p c t", t=CH)

        def at_step(t, i):
            return by_chunk(t)[:, :, i:i + 1].broadcast_to([P, NCH, CH])

        with nc.Block() as block:
            @block.sync
            def _(sp):
                load_mod(sp, io, AB[:, 0, :, :], 0, 1, mod_in)
                load_mod(sp, io, AB[:, 1, :, :], 0, 0, mod_in)
                sp.dma_start(lbr[:, :, :, :], io["hgrn_lb"]).then_inc(lb_in, 16)
                sp.dma_start(gn[:, :], io["gnormT"]).then_inc(gn_in, 16)
                sp.sem_inc(st_free, 1)
                with sp.Fori(0, HG) as h:
                    sp.wait_ge(proj[3], h + 1)
                    sp.dma_start(wh[:, :, :].rearrange("p k n -> p (k n)"),
                                 io["w_hgrn"][bass.ds(h, 1), :, :].rearrange("a p n -> (a p) n")).then_inc(wh_in, 16)
                    sp.wait_ge(head_done, h + 1)
                    sp.dma_start(S[0][:, 0, :], io["state0"][0, bass.ds(h, 1), :, :].rearrange("a p n -> (a p) n")).then_inc(s0_in, 16)
                    sp.dma_start(S[1][:, SCH - 1, :], io["state0"][1, bass.ds(h, 1), :, :].rearrange("a p n -> (a p) n")).then_inc(s0_in, 16)
                    sp.wait_ge(s_done, h * 2 + 2)
                    sp.dma_start(io["new_hf"][0, 0, bass.ds(h, 1), :, :].rearrange("a p n -> (a p) n"), S[0][:, NCH, :]).then_inc(st_out, 16)
                    sp.dma_start(io["new_hb"][0, 0, bass.ds(h, 1), :, :].rearrange("a p n -> (a p) n"), S[1][:, NCH, :]).then_inc(st_out, 16)
                    sp.wait_ge(st_out, h * 32 + 32)
                    sp.sem_inc(st_free, 1)
                sp.dma_start(watt[:, :, :].rearrange("p k n -> p (k n)"), io["w_att"]).then_inc(watt_in, 16)
                sp.wait_ge(st_out, 32 * HG)
                sp.wait_ge(watt_in, 16)

            @block.gpsimd
            def _(pool):
                c = Count(pool, consts)
                c.add(pool.memset(reset[:, :], 1.0))
                c.add(pool.memset(tri[:, :, :], 1.0))
                c.add(pool.memset(Vm[:, :, :, :], 0.0))
                for d in range(2):
                    c.add(pool.memset(AT[d][:, :], 0.0))
                    c.add(pool.memset(S[d][:, SCH + d * (NCH - SCH - 1), :], 0.0))
                c.wait()
                c.add(pool.memset(by_chunk(reset)[:, :, 0:1], 0.0))
                c.add(pool.affine_select(out=tri[:, 0, :], in_=tri[:, 0, :], compare_op=ALU.is_ge, fill=0.0,
                                         base=0, pattern=[[1, P]], channel_multiplier=-1))
                c.add(pool.affine_select(out=tri[:, 1, :], in_=tri[:, 1, :], compare_op=ALU.is_ge, fill=0.0,
                                         base=0, pattern=[[-1, P]], channel_multiplier=1))
                c.wait()
                c.add(pool.affine_select(out=tri[:, 0, CH:P], in_=tri[:, 0, CH:P], compare_op=ALU.is_ge, fill=0.0,
                                         base=-CH, pattern=[[0, CH]], channel_multiplier=1))
                c.add(pool.affine_select(out=tri[:, 1, 0:CH], in_=tri[:, 1, 0:CH], compare_op=ALU.is_ge, fill=0.0,
                                         base=CH - 1, pattern=[[0, CH]], channel_multiplier=-1))
                assert c.n == NCONST
                with pool.Fori(0, HG) as h:
                    pool.wait_ge(v_done, h * 2 + 2)
                    wait_apart(pool, u_done, h * 2 + 1)
                    for half in range(2):
                        rows = slice(half * CH, half * CH + CH)
                        pool.tensor_copy(Vm[rows, :, half, :], V[rows, :, :]).then_inc(vm_done, 1)

            @block.scalar
            def _(act):
                act.wait_ge(lb_step, 2)
                act.activation(lbe[:, :, :, :], lbe[:, :, :, :], ACT.Exp).then_inc(lb_exp, 1)
                n_act(act)
                act.wait_ge(lb_ready, 1)
                with act.Fori(0, HG) as h:
                    act.wait_ge(head_done, h + 1)
                    for d, (src, p) in enumerate(((D0, proj[0]), (D1, proj[1]))):
                        act.wait_ge(p, h + 1)
                        act.activation(G[d][:, :], src[:, 0:T], ACT.Sigmoid)
                        act.activation(K[d][:, :], src[:, 0:T], ACT.Sigmoid, scale=-1.0).then_inc(sig_done, 1)
                    act.wait_ge(proj[2], h + 1)
                    act.activation(SQ[:, :], D0[:, 0:T], ACT.Sigmoid).then_inc(sig_done, 1)
                    act.wait_ge(sig_done, h * 3 + 3)
                    for d in range(2):
                        act.activation(G[d][:, :], G[d][:, :], ACT.Ln, scale=oml[:, d, bass.ds(h, 1)],
                                       bias=lb[:, d, bass.ds(h, 1)]).then_inc(ln_done, 1)
                    for d in range(2):
                        act.wait_ge(diff_done, h * 4 + (2 * d + 2))
                        act.activation(QI[d][:, :], G[d][:, :], ACT.Exp)
                        act.activation(KI[d][:, :], G[d][:, :], ACT.Exp, scale=-1.0)
                        act.activation(QB[d][:, :], B[d][:, :], ACT.Exp)
                        act.activation(KL[d][:, :], KL[d][:, :], ACT.Exp).then_inc(exp_done, 1)
                    act.wait_ge(proj[3], h + 2)
                    vg = D1[:, :].rearrange("p (b n) -> p b n", n=2 * P)
                    act.activation(V[:, 0:SB, :], vg[:, :, 0:P], ACT.Copy).then_inc(v_done, 1)
                    act.activation(V[:, SB, :], D0[:, T:T + P], ACT.Copy).then_inc(v_done, 1)
                    act.activation(ZG[:, 0:SB, :], vg[:, :, P:2 * P], ACT.Sigmoid)
                    act.activation(ZG[:, SB, :], D0[:, T + P:T + 2 * P], ACT.Sigmoid).then_inc(zg_sig, 1)
                    for d, src in enumerate((D2, D3)):
                        act.wait_ge(klt_psum, h * 2 + (d + 1))
                        act.activation(KLT[d][:, :], src[:, 0:T], ACT.Copy).then_inc(klt_done, 1)
                    act.wait_ge(o_done, h + 1)
                    act.activation(ON[:, :, :].rearrange("p b v -> p (b v)"), D2[:, 0:T], ACT.Square).then_inc(o_sq, 1)
                    act.wait_ge(ss_done, h + 1)
                    act.activation(RT[:, :], SS[:, :], ACT.Sqrt).then_inc(rt_done, 1)

            @block.vector
            def _(dve):
                dve.sem_inc(head_done, 1)
                c = Count(dve, lb_step)
                dve.wait_ge(lb_in, 16)
                c.add(dve.tensor_tensor(lbx[:, :, :], lbr[:, :, 0, :], lbr[:, :, 1, :], ALU.max))
                c.wait()
                c.add(dve.tensor_tensor(lbe[:, :, :, :], lbr[:, :, :, :],
                                        lbx[:, :, :].unsqueeze(2).broadcast_to([P, 2, 2, HG]), ALU.subtract))
                dve.wait_ge(lb_exp, 1)
                c.add(dve.tensor_tensor(lbx[:, :, :], lbe[:, :, 0, :], lbe[:, :, 1, :], ALU.add))
                c.wait()
                c.add(dve.reciprocal(lbx[:, :, :], lbx[:, :, :]))
                c.wait()
                c.add(dve.tensor_tensor(lb[:, :, :], lbe[:, :, 0, :], lbx[:, :, :], ALU.mult))
                c.wait()
                dve.tensor_scalar(oml[:, :, :], lb[:, :, :], -1.0, 1.0, ALU.mult, ALU.add).then_inc(lb_ready, 1)
                n_dve(dve)
                dve.wait_ge(lb_ready, 1)
                dve.wait_ge(gn_in, 16)
                dve.wait_ge(consts, NCONST)
                with dve.Fori(0, HG) as h:
                    r = Count(dve, dstep, h * DSTEPS)
                    for d in range(2):
                        dve.wait_ge(sig_done, h * 3 + (d + 1))
                        r.add(dve.tensor_scalar(K[d][:, :], K[d][:, :], oml[:, d, bass.ds(h, 1)], None, ALU.mult))
                    dve.wait_ge(sig_done, h * 3 + 3)
                    dve.tensor_tensor(Q[:, :], D0[:, 0:T], SQ[:, :], ALU.mult).then_inc(q_made, 1)
                    for d in range(2):
                        dve.wait_ge(ln_done, h * 2 + (d + 1))
                        step = slice(None, None, -1) if d else slice(None)
                        r.add(dve.tensor_tensor_scan(B[d][:, step], reset[:, :], G[d][:, step], 0.0, ALU.mult, ALU.add))
                        r.wait()
                        dve.tensor_tensor(by_chunk(G[d]), by_chunk(B[d]), at_step(B[d], middle[d]),
                                          ALU.subtract).then_inc(diff_done, 1)
                        dve.tensor_tensor(by_chunk(KL[d]), at_step(B[d], final[d]), by_chunk(B[d]),
                                          ALU.subtract).then_inc(diff_done, 1)
                    dve.wait_ge(q_made, h + 1)
                    for d in range(2):
                        dve.wait_ge(exp_done, h * 2 + (d + 1))
                        r.add(dve.tensor_copy(EBL[:, d, :], by_chunk(QB[d])[:, :, final[d]]))
                        r.wait()
                        r.add(dve.tensor_tensor(QI[d][:, :], QI[d][:, :], Q[:, :], ALU.mult))
                        r.add(dve.tensor_tensor(KI[d][:, :], KI[d][:, :], K[d][:, :], ALU.mult))
                        r.add(dve.tensor_tensor(QB[d][:, :], QB[d][:, :], Q[:, :], ALU.mult))
                        r.wait()
                        dve.tensor_tensor(KL[d][:, :], KL[d][:, :], K[d][:, :], ALU.mult).then_inc(kl_done, 1)
                    dve.wait_ge(zg_sig, h + 1)
                    vg = D1[:, :].rearrange("p (b n) -> p b n", n=2 * P)
                    dve.tensor_tensor(ZG[:, 0:SB, :], ZG[:, 0:SB, :], vg[:, :, P:2 * P], ALU.mult).then_inc(vg_read, 1)
                    dve.tensor_tensor(ZG[:, SB, :], ZG[:, SB, :], D0[:, T + P:T + 2 * P], ALU.mult).then_inc(vg_read, 1)
                    for d, src in enumerate((D2, D3)):
                        wait_apart(dve, at_psum, h * 2 + (d + 1))
                        dve.copy_predicated(AT[d][:, :].rearrange("p (b t) -> p b t", t=P),
                                            tri[:, d, :].bitcast(U32).unsqueeze(1).broadcast_to([P, NB, P]),
                                            src[:, 0:T].rearrange("p (b t) -> p b t", t=P)).then_inc(at_done, 1)
                    dve.wait_ge(s0_in, h * 32 + 32)
                    dve.wait_ge(st_free, h + 1)

                    def advance(d, src, dst, chunk):
                        if chunk < SCH:
                            U = (D0, D1)[d][:, chunk * P:(chunk + 1) * P]
                        else:
                            U = (D2, D3)[d][:, T + (chunk - SCH) * P:T + (chunk - SCH + 1) * P]
                        return dve.scalar_tensor_tensor(out=S[d][:, dst, :], in0=S[d][:, src, :],
                                                        scalar=EBL[:, d, chunk:chunk + 1], in1=U,
                                                        op0=ALU.mult, op1=ALU.add)

                    dve.wait_ge(u_done, h * 2 + 3)
                    for i in range(SCH - 1):
                        r.add(advance(0, i, i + 1, i))
                        r.add(advance(1, SCH - 1 - i, SCH - 2 - i, SCH - 1 - i))
                        if i < 1:
                            r.add(advance(0, SCH, SCH + 1, SCH))
                            r.add(advance(1, NCH - 1, SCH, NCH - 1))
                        if i == 1:
                            advance(0, SCH + 1, NCH, NCH - 1).then_inc(s_done, 1)
                            advance(1, SCH, NCH, SCH).then_inc(s_done, 1)
                        if i < SCH - 2:
                            r.wait()
                    r.wait()
                    dve.sem_inc(states_done, 1)
                    dve.wait_ge(o_sq, h + 1)
                    r.add(dve.tensor_reduce(SS[:, :], ON[:, :, :], AX.X, ALU.add))
                    r.wait()
                    dve.tensor_scalar(SS[:, :], SS[:, :], 1.0 / P, EPS, ALU.mult, ALU.add).then_inc(ss_done, 1)
                    dve.wait_ge(rt_done, h + 1)
                    r.add(dve.reciprocal(RS[:, :], RT[:, :]))
                    r.wait()
                    r.add(dve.tensor_tensor(ON[:, :, :], D2[:, 0:T].rearrange("p (b v) -> p b v", v=P),
                                            RS[:, :].unsqueeze(2).broadcast_to([P, NB, P]), ALU.mult))
                    r.wait()
                    dve.tensor_tensor(ON[:, :, :], ON[:, :, :], ZG[:, :, :], ALU.mult).then_inc(on_done, 1)
                    dve.wait_ge(on_turned, h + 1)
                    dve.tensor_scalar(YT[:, :, bass.ds(h * P, P)], D3[:, 0:T].rearrange("p (b t) -> p b t", t=P),
                                      gn[:, bass.ds(h, 1)], None, ALU.mult).then_inc(head_done, 1)
                    assert r.n == DSTEPS, r.n

            @block.tensor
            def _(pe):
                pe.sem_inc(proj[3], 1)
                pe.sem_inc(u_done, 1)
                n_pe(pe)
                pe.wait_ge(h_stored, n_stored)
                pe.wait_ge(consts, NCONST)
                with pe.Fori(0, HG) as h:
                    def project(dst, col):
                        for lo, hi in ((0, LS), (LS, T)):
                            for k in range(KD):
                                last = pe.matmul(dst[:, lo:hi], wh[:, k, col * P:(col + 1) * P], HT[:, k, lo:hi],
                                                 start=(k == 0), stop=(k == KD - 1))
                        return last

                    pe.wait_ge(wh_in, h * 16 + 16)
                    pe.wait_ge(head_done, h + 1)
                    project(D0, 0).then_inc(proj[0], 1)
                    project(D1, 1).then_inc(proj[1], 1)
                    pe.wait_ge(sig_done, h * 3 + 1)
                    project(D0, 2).then_inc(proj[2], 1)
                    pe.wait_ge(sig_done, h * 3 + 2)
                    for b in range(NB):
                        dst = D1[:, b * 2 * P:(b + 1) * 2 * P] if b < SB else D0[:, T:T + 2 * P]
                        if b == SB:
                            pe.wait_ge(q_made, h + 1)
                        for k in range(KD):
                            last = pe.matmul(dst, HT[:, k, b * P:(b + 1) * P], wh[:, k, 3 * P:5 * P],
                                             start=(k == 0), stop=(k == KD - 1))
                    last.then_inc(proj[3], 1)
                    for d, dst in enumerate((D2, D3)):
                        pe.wait_ge(kl_done, h * 2 + (d + 1))
                        for b in range(NB):
                            last = pe.transpose(dst[:, b * P:(b + 1) * P], KL[d][:, b * P:(b + 1) * P], ident[:, :])
                        last.then_inc(klt_psum, 1)
                    for d, dst in enumerate((D2, D3)):
                        pe.wait_ge(klt_done, h * 2 + (d + 1))
                        for b in range(NB):
                            t = slice(b * P, (b + 1) * P)
                            last = pe.matmul(dst[:, t], KI[d][:, t], QI[d][:, t], start=True, stop=True)
                        last.then_inc(at_psum, 1)
                    pe.wait_ge(vm_done, h * 2 + 2)
                    pe.wait_ge(q_made, h + 1)
                    pe.wait_ge(vg_read, h * 2 + 2)
                    for d, (dst, extra) in enumerate(((D0, D2), (D1, D3))):
                        for b in range(NB):
                            out = dst[:, b * 2 * P:(b + 1) * 2 * P] if b < SB else extra[:, T:T + 2 * P]
                            if b == SB:
                                pe.wait_ge(at_done, h * 2 + (d + 1))
                            last = pe.matmul(out, KLT[d][:, b * P:(b + 1) * P],
                                             Vm[:, b, :, :].rearrange("p c v -> p (c v)"), start=True, stop=True)
                        last.then_inc(u_done, 1)
                    pe.wait_ge(at_done, h * 2 + 2)
                    pe.wait_ge(states_done, h + 1)
                    for b in range(NB):
                        t = slice(b * P, (b + 1) * P)
                        for d in range(2):
                            pe.matmul(D2[:, t], AT[d][:, t], V[:, b, :], start=(d == 0), stop=False,
                                      skip_group_check=True)
                        for half in range(2):
                            c = 2 * b + half
                            for d in range(2):
                                last = pe.matmul(D2[half * CH:(half + 1) * CH, t], QB[d][:, c * CH:(c + 1) * CH],
                                                 S[d][:, c, :], start=False, stop=(d == 1 and half == 1),
                                                 skip_group_check=True)
                    last.then_inc(o_done, 1)
                    pe.wait_ge(on_done, h + 1)
                    for b in range(NB):
                        last = pe.transpose(D3[:, b * P:(b + 1) * P], ON[:, b, :], ident[:, :])
                    last.then_inc(on_turned, 1)

    phase(nc, "hgrn", body)


def attention(nc, X, HT, YT, watt, ident, io):
    def body(sb, ps, sem):
        ROT = (2 * NG + 2) * HD
        cos = sb("cos", [P, SB, HD])
        sin = sb("sin", [P, SB, HD])
        QK = sb("QK", [P, NB, ROT])
        TR = sb("TR", [P, 2, ROT])
        VA = sb("VA", [P, NB, P])
        QT = sb("QT", [P, NG + 1, T])
        KT = QT[:, NG, :]
        QG = sb("QG", [P, T])
        CK = sb("CK", [P, P])
        CKT = sb("CKT", [P, P])
        CV = sb("CV", [P, P])
        band = sb("band", [P, 4, P])
        sink = sb("sink", [P, 2, NG])
        LG = sb("LG", [P, 2, 4 * P])
        PR = sb("PR", [P, 2, 4 * P])
        PT = sb("PT", [P, 2, 4 * P])
        mx = sb("mx", [P, 2 * NB])
        nm = sb("nm", [P, 2 * NB])
        den = sb("den", [P, 2 * NB])
        es = sb("es", [P, 2 * NB])
        rd = sb("rd", [P, 2 * NB])
        A = [ps(f"A{i}", 1024) for i in range(4)]
        L = [A[0][:, 0:512], A[0][:, 512:1024]]
        TP = [A[1][:, 0:512], A[1][:, 512:1024]]
        O = A[2]

        tables_in, ctx_in, sink_in, kv_out = sem("tables_in"), sem("ctx_in"), sem("sink_in"), sem("kv_out")
        mask_step, projected, evacuated = sem("mask_step"), sem("projected"), sem("evacuated")
        turned, t_stored, raw_k = sem("a_turned"), sem("a_stored"), sem("raw_k")
        rot_step, v_stored = sem("rot_step"), sem("v_stored")
        g_staged, lg_done, nm_done, exp_done = sem("g_staged"), sem("lg_done"), sem("nm_done"), sem("a_exp")
        pn_done, tp_done, pt_done, pv_done, o_stored = (sem(n) for n in ("pn_done", "tp_done", "pt_done", "pv_done", "o_stored"))
        astep = sem("astep")
        U = 2 * NB

        def spans(b):
            if b == SB:
                return [(2, KT[:, SB * P:T])]
            out = [(1, CKT[:, :])]
            if b > 0:
                out.insert(0, (0, KT[:, (b - 1) * P:b * P]))
            hi = min(b + 2, SB)
            out.append((2, KT[:, b * P:hi * P]))
            return out

        def columns(b):
            if b == SB:
                return 2, 3
            return (0 if b else 1), (4 if b < SB - 1 else 3)

        def values(b, n):
            if b == SB:
                return VA[:, SB, :]
            return CV[:, :] if n == 1 else VA[:, b + (-1, 0, 0, 1)[n], :]

        with nc.Block() as block:
            @block.sync
            def _(sp):
                sp.dma_start(cos[:, :, :], io["rope_cos"]).then_inc(tables_in, 16)
                sp.dma_start(sin[:, :, :], io["rope_sin"]).then_inc(tables_in, 16)
                sp.dma_start(CK[:, :], io["cache_k"].rearrange("b n s k d -> (b n s) (k d)")).then_inc(ctx_in, 16)
                sp.dma_start(CV[:, :], io["cache_v"].rearrange("b n s k d -> (b n s) (k d)")).then_inc(ctx_in, 16)
                sp.dma_start(sink[:, :, :].rearrange("p a g -> p (a g)"),
                             broadcast_rows(io["attn_sink"].rearrange("n h -> (n h)"), 0, 2 * NG)).then_inc(sink_in, 16)
                sp.wait_ge(raw_k, 1)
                sp.dma_start(io["new_k"].rearrange("b n s k d -> (b n s) (k d)"), QK[:, SB, 2 * NG * HD:ROT]).then_inc(kv_out, 16)
                sp.wait_ge(v_stored, NB)
                sp.dma_start(io["new_v"].rearrange("b n s k d -> (b n s) (k d)"), VA[:, SB, :]).then_inc(kv_out, 16)
                sp.wait_ge(kv_out, 32)

            @block.gpsimd
            def _(pool):
                pool.memset(band[:, :, :], 0.0).then_inc(mask_step, 1)
                pool.wait_ge(mask_step, 1)
                pool.affine_select(out=band[:, 0, :], in_=band[:, 0, :], compare_op=ALU.is_ge, fill=NEG,
                                   base=0, pattern=[[1, P]], channel_multiplier=-1).then_inc(mask_step, 1)
                pool.affine_select(out=band[:, 3, :], in_=band[:, 3, :], compare_op=ALU.is_ge, fill=NEG,
                                   base=0, pattern=[[-1, P]], channel_multiplier=1).then_inc(mask_step, 1)

            @block.scalar
            def _(act):
                act.wait_ge(projected, NB)
                act.activation(QK[:, SB, :], A[SB % 2][:, 0:ROT], ACT.Copy).then_inc(raw_k, 1)
                act.activation(VA[:, SB, :], A[SB % 2][:, ROT:ROT + P], ACT.Copy).then_inc(v_stored, 1)
                for b in range(NB):
                    act.wait_ge(turned, b + 1)
                    act.activation(QT[:, :, b * P:(b + 1) * P],
                                   A[2 + b % 2][:, 0:(NG + 1) * P].rearrange("p (g t) -> p g t", t=P), ACT.Copy).then_inc(t_stored, 1)
                act.wait_ge(turned, NB + 1)
                act.activation(CKT[:, :], A[2 + NB % 2][:, 0:P], ACT.Copy).then_inc(t_stored, 1)
                act.wait_ge(t_stored, NB + 1)
                act.wait_ge(sink_in, 16)
                act.sem_inc(o_stored, 1)
                with act.Fori(0, NG) as g:
                    act.wait_ge(pv_done, g * U + 1)
                    act.activation(QG[:, :], QT[:, bass.ds(g, 1), :].rearrange("p a t -> p (a t)"), ACT.Copy).then_inc(g_staged, 1)
                    for s in range(U + 1):
                        if s < U:
                            b, kv = divmod(s, 2)
                            lo, hi = columns(b)
                            c = slice(lo * P, hi * P)
                            act.wait_ge(nm_done, g * U + (s + 1))
                            act.activation(PR[:, s % 2, c], LG[:, s % 2, c], ACT.Exp, bias=nm[:, s:s + 1],
                                           accum_out=den[:, s:s + 1])
                            act.activation(es[:, s:s + 1], sink[:, kv, bass.ds(g, 1)], ACT.Exp,
                                           bias=nm[:, s:s + 1]).then_inc(exp_done, 1)
                        if s >= 1:
                            lo, hi = columns((s - 1) // 2)
                            c = slice(lo * P, hi * P)
                            act.wait_ge(tp_done, g * U + s)
                            act.activation(PT[:, (s - 1) % 2, c], TP[(s - 1) % 2][:, c], ACT.Copy).then_inc(pt_done, 1)
                    act.wait_ge(pv_done, g * U + (U + 1))
                    act.activation(YT[:, :, bass.ds(g * P + HG * P, P)],
                                   O[:, 0:T].rearrange("p (b t) -> p b t", t=P), ACT.Copy).then_inc(o_stored, 1)

            @block.vector
            def _(dve):
                dve.wait_ge(tables_in, 32)
                r = Count(dve, rot_step)
                for b in range(SB):
                    dve.wait_ge(projected, b + 1)
                    z = A[b % 2][:, 0:ROT]
                    n = ROT // HD
                    head = lambda t: t.rearrange("p (n d) -> p n d", d=HD)
                    quarter = lambda t: t.rearrange("p (n a w f) -> p n a w f", a=2, w=2, f=HD // 4)
                    table = lambda t: t[:, b, :].unsqueeze(1).broadcast_to([P, n, HD])
                    r.add(dve.tensor_tensor(head(TR[:, 0, :]), head(z), table(cos), ALU.mult))
                    for w in range(2):
                        sn = sin[:, b, :].rearrange("p (a w f) -> p a w f", a=2, w=2)[:, :, w, :]
                        r.add(dve.tensor_tensor(quarter(TR[:, 1, :])[:, :, :, w, :], quarter(z)[:, :, :, 1 - w, :],
                                                sn.unsqueeze(1).broadcast_to([P, n, 2, HD // 4]), ALU.mult))
                    dve.tensor_copy(VA[:, b, :], A[b % 2][:, ROT:ROT + P]).then_inc(v_stored, 1)
                    r.wait()
                    dve.tensor_tensor(QK[:, b, :], TR[:, 0, :], TR[:, 1, :], ALU.add).then_inc(evacuated, 1)
                    dve.wait_ge(evacuated, b + 1)
                dve.wait_ge(mask_step, 3)
                dve.wait_ge(sink_in, 16)
                with dve.Fori(0, NG) as g:
                    r = Count(dve, astep, g * (3 * U))
                    for s in range(U + 1):
                        if s < U:
                            b, kv = divmod(s, 2)
                            lo, hi = columns(b)
                            c = slice(lo * P, hi * P)
                            wait_apart(dve, lg_done, g * U + (s + 1))
                            r.add(dve.tensor_tensor_reduce(LG[:, s % 2, c], L[kv][:, c],
                                                           band[:, :, :].rearrange("p a k -> p (a k)")[:, c],
                                                           SCALE, -3e38, ALU.add, ALU.max, mx[:, s:s + 1]))
                            r.wait()
                            dve.tensor_scalar(nm[:, s:s + 1], mx[:, s:s + 1], sink[:, kv, bass.ds(g, 1)], -1.0,
                                              ALU.max, ALU.mult).then_inc(nm_done, 1)
                        if s >= 1:
                            q = s - 1
                            lo, hi = columns(q // 2)
                            c = slice(lo * P, hi * P)
                            dve.wait_ge(exp_done, g * U + s)
                            r.add(dve.tensor_tensor(rd[:, q:q + 1], den[:, q:q + 1], es[:, q:q + 1], ALU.add))
                            r.wait()
                            r.add(dve.reciprocal(rd[:, q:q + 1], rd[:, q:q + 1]))
                            r.wait()
                            dve.tensor_scalar(PR[:, q % 2, c], PR[:, q % 2, c], rd[:, q:q + 1], None,
                                              ALU.mult).then_inc(pn_done, 1)
                    assert r.n == 3 * U

            @block.tensor
            def _(pe):
                for b in range(NB):
                    if b >= 2:
                        pe.wait_ge(evacuated, b - 1)
                        pe.wait_ge(v_stored, b - 1)
                    for lo, hi in ((0, 512), (512, ROT + P)):
                        for k in range(KD):
                            last = pe.matmul(A[b % 2][:, lo:hi], HT[:, k, b * P:(b + 1) * P], watt[:, k, lo:hi],
                                             start=(k == 0), stop=(k == KD - 1))
                    last.then_inc(projected, 1)
                pe.wait_ge(ctx_in, 32)
                for b in range(NB):
                    if b < SB:
                        pe.wait_ge(evacuated, b + 1)
                    else:
                        pe.wait_ge(raw_k, 1)
                    if b >= 2:
                        pe.wait_ge(t_stored, b - 1)
                    for i in range(NG + 1):
                        last = pe.transpose(A[2 + b % 2][:, i * P:(i + 1) * P], QK[:, b, i * P:(i + 1) * P], ident[:, :])
                    last.then_inc(turned, 1)
                pe.wait_ge(t_stored, NB - 1)
                pe.transpose(A[2 + NB % 2][:, 0:P], CK[:, :], ident[:, :]).then_inc(turned, 1)
                pe.wait_ge(t_stored, NB + 1)
                pe.wait_ge(v_stored, NB)
                pe.sem_inc(pv_done, 1)
                with pe.Fori(0, NG) as g:
                    pe.wait_ge(g_staged, g + 1)

                    def logits(s):
                        b, kv = divmod(s, 2)
                        rows = slice(kv * HD, (kv + 1) * HD)
                        if s >= 2:
                            pe.wait_ge(nm_done, g * U + (s - 1))
                        for n, keys in spans(b):
                            cols = keys.shape[1]
                            last = pe.matmul(L[kv][:, n * P:n * P + cols], QG[rows, b * P:(b + 1) * P], keys[rows, :],
                                             start=True, stop=True)
                        last.then_inc(lg_done, 1)

                    logits(0)
                    logits(1)
                    for s in range(1, U + 2):
                        if s + 1 < U:
                            logits(s + 1)
                        if s <= U:
                            q = s - 1
                            pe.wait_ge(pn_done, g * U + s)
                            for n in range(*columns(q // 2)):
                                last = pe.transpose(TP[q % 2][:, n * P:(n + 1) * P], PR[:, q % 2, n * P:(n + 1) * P], ident[:, :])
                            last.then_inc(tp_done, 1)
                        if s >= 2:
                            q = s - 2
                            b, kv = divmod(q, 2)
                            pe.wait_ge(pt_done, g * U + (q + 1))
                            if q == 0:
                                pe.wait_ge(o_stored, g + 1)
                            lo, hi = columns(b)
                            for n in range(lo, hi):
                                last = pe.matmul(O[kv * HD:(kv + 1) * HD, b * P:(b + 1) * P],
                                                 values(b, n)[:, kv * HD:(kv + 1) * HD], PT[:, q % 2, n * P:(n + 1) * P],
                                                 start=(n == lo), stop=(n == hi - 1))
                            last.then_inc(pv_done, 1)

    phase(nc, "att", body)


def even_mixer(nc, X, HT, YT, ident, io):
    with ExitStack() as ctx:
        watt = ctx.enter_context(nc.sbuf_tensor("watt", [P, KD, 6 * P], F32))
        hgrn(nc, X, HT, YT, watt, ident, io)
        attention(nc, X, HT, YT, watt, ident, io)


def rglru(nc, X, HT, YT, ident, io):
    def body(sb, ps, sem):
        NPAR, NCOL = 13, 17
        TAPS, CB, BA, BX, LAM, H0, CA, CT = 0, 4, 5, 7, 9, 11, 13, 15
        W = KD // RB
        XP = T + 6
        w = sb("wlru", [P, KD, 4 * P])
        wrg = sb("wrg", [P, W, 4, W * P])
        AB = sb("ABo", [P, 2, 2, D])
        chan = sb("chan", [P, KD, NCOL])
        par = sb("par", [P, W, NCOL])
        sp_y = sb("sp_y", [P, KD, 2])
        sp_m = sb("sp_m", [P, KD, 2])
        sp_z = sb("sp_z", [P, KD, 2])
        sp_s = sb("sp_s", [P, KD, 2])
        sp_p = sb("sp_p", [P, KD, 2])
        ends = sb("ends", [P, 2, KD])
        endsT = sb("endsT", [2 * KD, P])
        xp = [sb(f"xp{c}", [P, XP]) for c in range(W)]
        cv = [sb(f"cv{c}", [P, T + 3]) for c in range(W)]
        xc = [sb(f"xc{c}", [P, T]) for c in range(W)]
        GT = [sb(f"GT{c}", [P, T]) for c in range(W)]
        R, I, AA, HH = ([[sb(f"{n}{d}{c}", [P, T]) for c in range(W)] for d in range(2)] for n in ("R", "I", "AA", "HH"))
        Dp = [ps(f"D{i}", 1024) for i in range(4)]

        mod_in, chan_in = sem("l_mod_in"), sem("chan_in")
        n_act, n_dve, n_pe, h_stored, n_stored = norm_parts(sb, sem, "l_", X, YT, HT, ident, AB, mod_in, 64, Dp[2][:, :], Dp[0:2])
        pads, sp_step, sp_exp, sp_ready = sem("pads"), sem("sp_step"), sem("sp_exp"), sem("sp_ready")
        w_in, wrg_in = sem("wlru_in"), sem("wrg_in")
        xr_done, gt_done, rg_done = sem("xr_done"), sem("gt_done"), sem("rg_done")
        xp_done, gelu_done, sig_done, ex_done, sq_done = (sem(n) for n in ("xp_done", "gelu_done", "l_sig", "l_ex", "sq_done"))
        conv_done, m_done, y_done, lstep = sem("conv_done"), sem("m_done"), sem("l_y"), sem("lstep")
        ends_turned, ends_stored, ends_out = sem("ends_turned"), sem("ends_stored"), sem("ends_out")
        LSTEPS = 1 + W * 3 + 2 * W * 2 + 2 * W * 2 + 2 * W * 2 + W

        with nc.Block() as block:
            @block.sync
            def _(sp):
                load_mod(sp, io, AB[:, 0, :, :], 1, 1, mod_in)
                load_mod(sp, io, AB[:, 1, :, :], 1, 0, mod_in)
                sp.dma_start(chan[:, :, 0:NPAR], io["channels"]).then_inc(chan_in, 16)
                with sp.Fori(0, RB) as n:
                    sp.wait_ge(gt_done, n * W + 1)
                    sp.dma_start(w[:, :, :].rearrange("p k n -> p (k n)"),
                                 io["w_lru"][bass.ds(n, 1), :, :].rearrange("a p n -> (a p) n")).then_inc(w_in, 16)
                    sp.wait_ge(rg_done, n * (4 * W) + 1)
                    sp.dma_start(wrg[:, :, :, :].rearrange("p k m n -> p (k m n)"),
                                 io["w_rg"][bass.ds(n, 1), :, :].rearrange("a p n -> (a p) n")).then_inc(wrg_in, 16)
                sp.wait_ge(ends_stored, 1)
                for d, name in enumerate(("new_lf", "new_lb")):
                    sp.dma_start(io[name].rearrange("b n (k p) -> (b n k) p", p=P), endsT[d * KD:(d + 1) * KD, :]).then_inc(ends_out, 16)
                sp.wait_ge(ends_out, 32)

            @block.gpsimd
            def _(pool):
                for c in range(W):
                    for lo, hi in ((0, 2), (LS + 2, LS + 5), (XP - 1, XP)):
                        pool.memset(xp[c][:, lo:hi], 0.0).then_inc(pads, 1)

            @block.scalar
            def _(act):
                act.wait_ge(sp_step, 3)
                act.activation(sp_y[:, :, :], sp_y[:, :, :], ACT.Exp, scale=-1.0).then_inc(sp_exp, 1)
                n_act(act)
                with act.Fori(0, RB) as n:
                    for c in range(W):
                        act.wait_ge(xr_done, n * W + (c + 1))
                        act.activation(xp[c][:, 2:LS + 2], Dp[c][:, 0:LS], ACT.Copy)
                        act.activation(xp[c][:, LS + 5:XP - 1], Dp[c][:, LS:T], ACT.Copy).then_inc(xp_done, 1)
                    act.wait_ge(y_done, n * W + 1)
                    for c in range(W):
                        act.wait_ge(gt_done, n * W + (c + 2))
                        act.activation(GT[c][:, :], Dp[2 + c][:, 0:T], ACT.Gelu_apprx_tanh).then_inc(gelu_done, 1)
                    act.wait_ge(conv_done, n * W + W)
                    i = 0
                    for d in range(2):
                        for c in range(W):
                            for dst, bias in ((R, BA), (I, BX)):
                                act.wait_ge(rg_done, n * (4 * W) + (i + 2))
                                act.activation(dst[d][c][:, :], Dp[i % 4][:, 0:T], ACT.Sigmoid,
                                               bias=par[:, c, bias + d:bias + d + 1]).then_inc(sig_done, 1)
                                i += 1
                    act.wait_ge(sig_done, n * (4 * W) + (4 * W + 1))
                    for d in range(2):
                        for c in range(W):
                            act.activation(AA[d][c][:, :], R[d][c][:, :], ACT.Exp, scale=par[:, c, CA + d:CA + d + 1])
                            act.activation(R[d][c][:, :], R[d][c][:, :], ACT.Tanh,
                                           scale=par[:, c, CT + d:CT + d + 1]).then_inc(ex_done, 1)
                    for d in range(2):
                        for c in range(W):
                            act.wait_ge(m_done, n * (2 * W) + (d * W + c + 1))
                            act.activation(R[d][c][:, :], R[d][c][:, :], ACT.Sqrt).then_inc(sq_done, 1)
                act.wait_ge(ends_turned, 1)
                act.activation(endsT[:, :], Dp[0][0:2 * KD, 0:P], ACT.Copy).then_inc(ends_stored, 1)

            @block.vector
            def _(dve):
                dve.sem_inc(y_done, 1)
                c = Count(dve, sp_step)
                lam = chan[:, :, LAM:LAM + 2]
                dve.wait_ge(chan_in, 16)
                c.add(dve.tensor_scalar(sp_s[:, :, :], lam, -1.0, None, ALU.mult))
                c.wait()
                c.add(dve.tensor_scalar(sp_m[:, :, :], sp_s[:, :, :], 0.0, None, ALU.max))
                c.add(dve.tensor_tensor(sp_y[:, :, :], lam, sp_s[:, :, :], ALU.max))
                dve.wait_ge(sp_exp, 1)
                c.add(dve.tensor_scalar(sp_z[:, :, :], sp_y[:, :, :], 2.0, None, ALU.add))
                c.wait()
                c.add(dve.reciprocal(sp_z[:, :, :], sp_z[:, :, :]))
                c.wait()
                c.add(dve.tensor_tensor(sp_z[:, :, :], sp_z[:, :, :], sp_y[:, :, :], ALU.mult))
                c.wait()
                c.add(dve.tensor_tensor(sp_s[:, :, :], sp_z[:, :, :], sp_z[:, :, :], ALU.mult))
                c.wait()
                c.add(dve.tensor_scalar(sp_p[:, :, :], sp_s[:, :, :], 1.0 / 19, None, ALU.mult))
                for k in range(17, 1, -2):
                    c.wait()
                    c.add(dve.scalar_tensor_tensor(out=sp_p[:, :, :], in0=sp_p[:, :, :], scalar=1.0 / k, in1=sp_s[:, :, :],
                                                   op0=ALU.add, op1=ALU.mult))
                c.wait()
                c.add(dve.scalar_tensor_tensor(out=sp_p[:, :, :], in0=sp_p[:, :, :], scalar=1.0, in1=sp_z[:, :, :],
                                               op0=ALU.add, op1=ALU.mult))
                c.wait()
                c.add(dve.scalar_tensor_tensor(out=sp_p[:, :, :], in0=sp_p[:, :, :], scalar=2.0, in1=sp_m[:, :, :],
                                               op0=ALU.mult, op1=ALU.add))
                c.wait()
                dve.tensor_scalar(chan[:, :, CA:CA + 2], sp_p[:, :, :], -8.0, None, ALU.mult).then_inc(sp_ready, 1)
                dve.tensor_scalar(chan[:, :, CT:CT + 2], sp_p[:, :, :], 8.0, None, ALU.mult).then_inc(sp_ready, 1)
                n_dve(dve)
                dve.wait_ge(sp_ready, 2)
                dve.wait_ge(pads, 3 * W)
                with dve.Fori(0, RB) as n:
                    r = Count(dve, lstep, n * LSTEPS)
                    r.add(dve.tensor_copy(par[:, :, :], chan[:, bass.ds(n * W, W), :]))
                    r.wait()
                    for c in range(W):
                        dve.wait_ge(xp_done, n * W + (c + 1))
                        r.add(dve.tensor_scalar(cv[c][:, :], xp[c][:, 0:T + 3], par[:, c, TAPS:TAPS + 1],
                                                par[:, c, CB:CB + 1], ALU.mult, ALU.add))
                        r.wait()
                        for tap in (1, 2):
                            r.add(dve.scalar_tensor_tensor(out=cv[c][:, :], in0=xp[c][:, tap:tap + T + 3],
                                                           scalar=par[:, c, TAPS + tap:TAPS + tap + 1], in1=cv[c][:, :],
                                                           op0=ALU.mult, op1=ALU.add))
                            r.wait()
                        for lo, hi, at in ((0, LS, 0), (LS, T, 3)):
                            last = dve.scalar_tensor_tensor(out=xc[c][:, lo:hi], in0=xp[c][:, lo + at + 3:hi + at + 3],
                                                            scalar=par[:, c, TAPS + 3:TAPS + 4], in1=cv[c][:, lo + at:hi + at],
                                                            op0=ALU.mult, op1=ALU.add)
                        last.then_inc(conv_done, 1)
                    dve.wait_ge(conv_done, n * W + W)
                    for d in range(2):
                        for c in range(W):
                            dve.wait_ge(ex_done, n * (2 * W) + (d * W + c + 1))
                            r.add(dve.tensor_tensor(HH[d][c][:, :], AA[d][c][:, :], AA[d][c][:, :], ALU.mult))
                            r.add(dve.tensor_tensor(I[d][c][:, :], I[d][c][:, :], xc[c][:, :], ALU.mult))
                            r.wait()
                            dve.scalar_tensor_tensor(out=R[d][c][:, :], in0=HH[d][c][:, :], scalar=1.0, in1=R[d][c][:, :],
                                                     op0=ALU.add, op1=ALU.mult).then_inc(m_done, 1)
                    for d in range(2):
                        for c in range(W):
                            dve.wait_ge(sq_done, n * (2 * W) + (d * W + c + 1))
                            r.add(dve.tensor_tensor(I[d][c][:, :], I[d][c][:, :], R[d][c][:, :], ALU.mult))
                            r.wait()
                            for k, (lo, hi, h0) in enumerate(((0, LS, par[:, c, H0 + d:H0 + d + 1]), (LS, T, 0.0))):
                                t = slice(hi - 1, lo - 1 if lo else None, -1) if d else slice(lo, hi)
                                ins = dve.tensor_tensor_scan(HH[d][c][:, t], AA[d][c][:, t], I[d][c][:, t], h0,
                                                             ALU.mult, ALU.add)
                                r.add(ins)
                            r.wait()
                            end = LS if d else T - 1
                            r.add(dve.tensor_copy(ends[:, d, bass.ds(n * W + c, 1)], HH[d][c][:, end:end + 1]))
                    for c in range(W):
                        r.add(dve.tensor_tensor(HH[0][c][:, :], HH[0][c][:, :], HH[1][c][:, :], ALU.add))
                    r.wait()
                    dve.wait_ge(gelu_done, n * W + W)
                    for c in range(W):
                        dve.tensor_tensor(YT[:, :, bass.ds((n * W + c) * P, P)],
                                          HH[0][c][:, :].rearrange("p (b t) -> p b t", t=P),
                                          GT[c][:, :].rearrange("p (b t) -> p b t", t=P), ALU.mult).then_inc(y_done, 1)
                    assert r.n == LSTEPS, r.n

            @block.tensor
            def _(pe):
                for s in (gt_done, rg_done, sig_done):
                    pe.sem_inc(s, 1)
                n_pe(pe)
                pe.wait_ge(h_stored, n_stored)
                with pe.Fori(0, RB) as n:
                    pe.wait_ge(w_in, n * 16 + 16)
                    pe.wait_ge(sig_done, n * (4 * W) + 1)
                    for part, done in ((0, xr_done), (1, gt_done)):
                        for c in range(W):
                            for lo, hi in ((0, LS), (LS, T)):
                                for k in range(KD):
                                    last = pe.matmul(Dp[2 * part + c][:, lo:hi], w[:, k, (part * W + c) * P:(part * W + c + 1) * P],
                                                     HT[:, k, lo:hi], start=(k == 0), stop=(k == KD - 1))
                            last.then_inc(done, 1)
                    pe.wait_ge(wrg_in, n * 16 + 16)
                    pe.wait_ge(conv_done, n * W + W)
                    i = 0
                    for d in range(2):
                        for c in range(W):
                            for ax in range(2):
                                if i == 2:
                                    pe.wait_ge(gelu_done, n * W + W)
                                if i >= 4:
                                    pe.wait_ge(sig_done, n * (4 * W) + (i - 4 + 2))
                                for lo, hi in ((0, LS), (LS, T)):
                                    for k in range(W):
                                        last = pe.matmul(Dp[i % 4][:, lo:hi], wrg[:, k, 2 * d + ax, c * P:(c + 1) * P],
                                                         xc[k][:, lo:hi], start=(k == 0), stop=(k == W - 1))
                                last.then_inc(rg_done, 1)
                                i += 1
                pe.wait_ge(lstep, RB * LSTEPS)
                pe.wait_ge(sig_done, RB * 4 * W + 1)
                pe.transpose(Dp[0][0:2 * KD, 0:P], ends[:, :, :].rearrange("p d k -> p (d k)"), ident[:, :]).then_inc(ends_turned, 1)

    phase(nc, "lru", body)


def finish(nc, X, io):
    def body(sb, ps, sem):
        fg = sb("fg", [P, D])
        Y = sb("Y", [P, NB, D])
        junk = sb("junkf", [P, D])
        ss, rt, rs = sb("ssf", [P, NB]), sb("rtf", [P, NB]), sb("rsf", [P, NB])
        fg_in, squared, rooted, inverted = sem("fg_in"), sem("squaredf"), sem("rootedf"), sem("invertedf")
        y_done, y_out = sem("y_done"), sem("y_out")
        with nc.Block() as block:
            @block.sync
            def _(sp):
                sp.dma_start(fg[:, :], broadcast_rows(io["final_g"], 0, D)).then_inc(fg_in, 16)
                for b in range(NB):
                    sp.wait_ge(y_done, b + 1)
                    dst = io["y_sample"][0, b * P:(b + 1) * P, :] if b < SB else io["y_prompt"][0, :, :]
                    sp.dma_start(dst, Y[:, b, :]).then_inc(y_out, 16)
                sp.wait_ge(y_out, 16 * NB)

            @block.scalar
            def _(act):
                for b in range(NB):
                    if b:
                        act.wait_ge(squared, b)
                    act.activation(junk[:, :], X[:, b, :], ACT.Square, accum_out=ss[:, b:b + 1]).then_inc(squared, 1)
                act.wait_ge(squared, NB)
                act.activation(rt[:, :], ss[:, :], ACT.Copy, scale=1.0 / D, bias=EPS).then_inc(rooted, 1)
                act.wait_ge(rooted, 1)
                act.activation(rt[:, :], rt[:, :], ACT.Sqrt).then_inc(rooted, 1)

            @block.vector
            def _(dve):
                dve.wait_ge(rooted, 2)
                dve.reciprocal(rs[:, :], rt[:, :]).then_inc(inverted, 1)
                dve.wait_ge(inverted, 1)
                dve.wait_ge(fg_in, 16)
                for b in range(NB):
                    dve.scalar_tensor_tensor(out=Y[:, b, :], in0=X[:, b, :], scalar=rs[:, b:b + 1],
                                             in1=fg[:, :], op0=ALU.mult, op1=ALU.mult).then_inc(y_done, 1)

    phase(nc, "fin", body)


def build(nc, io):
    with ExitStack() as ctx:
        X = ctx.enter_context(nc.sbuf_tensor("X", [P, NB, D], F32))
        ident = ctx.enter_context(nc.sbuf_tensor("ident", [P, P], F32))
        iota16 = ctx.enter_context(nc.sbuf_tensor("iota16", [P, TOPK], F32))
        HY = ctx.enter_context(nc.sbuf_tensor("HY", [P, NB, D], F32))
        HT = ctx.enter_context(nc.sbuf_tensor("HT", [P, KD, T], F32))
        constants(nc, iota16)
        for name in PHASES:
            if name == "mod":
                modulation(nc, X, ident, io)
            elif name == "even":
                even_mixer(nc, X, HT, HY, ident, io)
            elif name == "odd":
                rglru(nc, X, HT, HY, ident, io)
            else:
                project_and_peer(nc, X, HY, HT, ident, iota16, int(name[-1]), io)
        finish(nc, X, io)


def constants(nc, iota16):
    with nc.Block() as block:
        @block.gpsimd
        def _(pool):
            pool.iota(iota16[:, :], pattern=[[1, TOPK]], base=0, channel_multiplier=0,
                      allow_small_or_imprecise_dtypes=True)


def lay_out(a):
    def tiles(w, n):
        k, cols = w.shape
        return np.ascontiguousarray(w.reshape(k // P, P, cols // n, n).transpose(2, 1, 0, 3)).reshape(cols // n, P, -1)

    out = {k: a[k] for k in ("x_prompt", "x_sample", "b_mod", "norm1_g", "norm2_g", "final_g", "cache_k", "cache_v",
                             "attn_sink")}
    w = a["w_in_even"][0]
    n = HG * P
    out["w_hgrn"] = np.stack([tiles(np.concatenate([w[:, s * n + h * P:s * n + (h + 1) * P] for s in (1, 2, 0, 3, 4)],
                                                   axis=1), 5 * P)[0] for h in range(HG)])
    wq = w[:, 5 * n:5 * n + 2 * NG * HD].reshape(D, 2, NG, HD).transpose(0, 2, 1, 3).reshape(D, -1)
    out["w_att"] = tiles(np.concatenate([wq, w[:, 5 * n + 2 * NG * HD:]], axis=1), 6 * P)[0]
    wo = a["w_out_even"][0]
    wo = np.concatenate([wo[:n], wo[n:].reshape(2, NG, HD, D).transpose(1, 0, 2, 3).reshape(-1, D)])
    out["w_out"] = np.stack([wo, a["w_out_odd"][0]])
    lb = np.stack([a["hgrn_lb_fwd"], a["hgrn_lb_bwd"]])
    out["hgrn_lb"] = np.ascontiguousarray(lb.reshape(2, 2, HG, P).transpose(3, 0, 1, 2))
    out["gnormT"] = np.ascontiguousarray(a["hgrn_gnorm_g"].reshape(HG, P).T)
    out["state0"] = np.stack([a["state_hgrn_fwd"][0, 0], a["state_hgrn_bwd"][0, 0]])
    ch = np.concatenate([a["conv_w"][0], a["conv_b"], a["rg_b_a"][0], a["rg_b_x"][0], a["rg_lambda"][0],
                         a["state_lru_fwd"][0], a["state_lru_bwd"][0]])
    out["channels"] = np.ascontiguousarray(ch.reshape(13, KD, P).transpose(2, 1, 0))
    wi = a["w_in_odd"][0]
    out["w_lru"] = np.stack([tiles(np.concatenate([wi[:, D + n * 256:D + (n + 1) * 256], wi[:, n * 256:(n + 1) * 256]],
                                                  axis=1), 4 * P)[0] for n in range(RB)])
    rg = np.stack([a["rg_w_a"][0], a["rg_w_x"][0]], axis=1)
    out["w_rg"] = np.ascontiguousarray(rg.reshape(4, RB, 2, P, 256).transpose(1, 3, 2, 0, 4)).reshape(RB, P, -1)
    t = np.arange(LS)
    inv = (1.0 / (np.float32(10000.0) ** (np.arange(HD // 4, dtype=np.float32) / np.float32(HD // 4)))).astype(np.float32)
    pos = np.stack([t // 64, t % 64], axis=1).astype(np.float32)
    ang = pos[:, :, None] * inv
    cos = np.stack([np.cos(ang)] * 2, axis=2)
    sin = np.stack([-np.sin(ang), np.sin(ang)], axis=2)
    for name, table in (("rope_cos", cos), ("rope_sin", sin)):
        out[name] = np.ascontiguousarray(table.reshape(SB, P, HD).transpose(1, 0, 2)).astype(np.float32)
    cond = np.stack([a["c"][0], a["c_ctx"]])
    out["condT"] = np.ascontiguousarray(cond.reshape(2, KD, P).transpose(2, 1, 0))
    out["w_mod"] = np.concatenate([tiles(a["w_mod"][l], 512) for l in range(LAYERS)])
    out["w_q"] = np.concatenate([tiles(a["peer_w_q"][l], 2 * P) for l in range(LAYERS)])
    out["keysT"] = np.ascontiguousarray(a["peer_keys"].transpose(0, 2, 4, 1, 3)).reshape(LAYERS * HEADS, P, 2 * NK)
    out["uv"] = np.concatenate([a["peer_u"], a["peer_v"]], axis=2).reshape(LAYERS * EXPERTS, 2 * D)
    return out


OUTS = [("y_prompt", (1, LP, D)), ("y_sample", (1, LS, D)), ("new_k", (1, 1, LP, 2, HD)), ("new_v", (1, 1, LP, 2, HD)),
        ("new_hf", (1, 1, HG, P, P)), ("new_hb", (1, 1, HG, P, P)), ("new_lf", (1, 1, D)), ("new_lb", (1, 1, D))]


def kernel(**inputs):
    import concourse.bacc as bacc
    from concourse.bass_utils import run_bass_kernel_spmd

    nc = bacc.Bacc("TRN2", target_bir_lowering=False, num_devices=1)
    arrays = lay_out({k: np.asarray(v) for k, v in inputs.items()})
    io, given = {}, {}
    for name, a in arrays.items():
        given["in_" + name] = a
        io[name] = nc.dram_tensor("in_" + name, a.shape, mybir.dt.from_np(a.dtype), kind="ExternalInput").ap()
    for name, shape in OUTS:
        io[name] = nc.dram_tensor("out_" + name, shape, F32, kind="ExternalOutput").ap()
    io["mod_rows"] = nc.dram_tensor("scratch_mod_rows", (2 * LAYERS * 6 * D,), F32, kind="Internal").ap()
    build(nc, io)
    r = run_bass_kernel_spmd(nc, [given], core_ids=[0])
    return tuple(r.results[0]["out_" + name] for name, _ in OUTS)
```

```python
from contextlib import ExitStack

import numpy as np

import concourse.bass as bass
from concourse import mybir

F32 = mybir.dt.float32
F32R = mybir.dt.float32r
U32 = mybir.dt.uint32
ALU = mybir.AluOpType
ACT = mybir.ActivationFunctionType
AX = mybir.AxisListType

P = 128
D = 1024
KD = D // P
LP, LS = 128, 512
T = LP + LS
NB = T // P
SB = LS // P
EPS = 1e-6
NEG = -1e30
LAYERS = 2
HEADS, NK, TOPK, EXPERTS = 8, 128, 16, 16384
SLOTS = 10
NDIAG = 4
PER_HEAD = NB * TOPK
HG, CH = 4, 64
NCH = T // CH
SCH = LS // CH
NG, HD = 4, 64
SCALE = HD ** -0.5
RB = 4


def cond_of(b):
    return 0 if b < SB else 1


def wait_apart(eng, sem, value):
    eng.wait_ge(sem, value)
    eng.nop(nofuse=True)


class Count:

    def __init__(self, eng, sem, base=0, apart=False):
        self.eng, self.sem, self.base, self.n, self.apart = eng, sem, base, 0, apart

    def add(self, ins):
        ins.then_inc(self.sem, 1)
        self.n += 1

    def wait(self):
        self.eng.wait_ge(self.sem, self.base + self.n)
        if self.apart:
            self.eng.nop(nofuse=True)


def broadcast_rows(ap, lo, n):
    return ap[lo:lo + n].unsqueeze(0).broadcast_to([P, n])


def phase(nc, name, body):
    with ExitStack() as ctx:
        def sb(what, shape, dt=F32):
            return ctx.enter_context(nc.sbuf_tensor(f"{name}_{what}", shape, dt))

        def ps(what, cols):
            return ctx.enter_context(nc.psum_tensor(f"{name}_{what}", [P, cols], F32))

        used = []

        def sem(what):
            used.append(ctx.enter_context(nc.semaphore(f"{name}_{what}")))
            return used[-1]

        body(sb, ps, sem)

        with nc.Block() as block:
            @block.gpsimd
            def _(pool):
                numbers = sorted(one.num for one in used)
                start = numbers[0]
                for n, after in zip(numbers, numbers[1:] + [None]):
                    if after != n + 1:
                        pool.sem_clear(range(start, n + 1))
                        start = after


def norm_parts(sb, sem, pre, X, H, HT, ident, AB, ab_landed, ab_target, junk, tp):
    ss = sb(pre + "ss", [P, NB])
    rt = sb(pre + "rt", [P, NB])
    rs = sb(pre + "rs", [P, NB])
    squared, rooted, inverted = sem(pre + "squared"), sem(pre + "rooted"), sem(pre + "inverted")
    scaled, ready = sem(pre + "scaled"), sem(pre + "h_ready")
    turned, stored = sem(pre + "turned"), sem(pre + "stored")

    def act(eng):
        for b in range(NB):
            if b:
                eng.wait_ge(squared, b)
            eng.activation(junk, X[:, b, :], ACT.Square, accum_out=ss[:, b:b + 1]).then_inc(squared, 1)
        eng.wait_ge(squared, NB)
        eng.activation(rt[:, :], ss[:, :], ACT.Copy, scale=1.0 / D, bias=EPS).then_inc(rooted, 1)
        eng.wait_ge(rooted, 1)
        eng.activation(rt[:, :], rt[:, :], ACT.Sqrt).then_inc(rooted, 1)
        for b in range(NB):
            eng.wait_ge(turned, b + 1)
            eng.activation(HT[:, :, b * P:(b + 1) * P], tp[b % 2][:, :].rearrange("p (k t) -> p k t", k=KD),
                           ACT.Copy).then_inc(stored, 1)

    def dve(eng):
        eng.wait_ge(rooted, 2)
        eng.reciprocal(rs[:, :], rt[:, :]).then_inc(inverted, 1)
        eng.wait_ge(inverted, 1)
        eng.wait_ge(ab_landed, ab_target)
        for b in range(NB):
            c = cond_of(b)
            eng.scalar_tensor_tensor(out=H[:, b, :], in0=X[:, b, :], scalar=rs[:, b:b + 1],
                                     in1=AB[:, 0, c, :], op0=ALU.mult, op1=ALU.mult).then_inc(scaled, 1)
            eng.wait_ge(scaled, b + 1)
            eng.tensor_tensor(H[:, b, :], H[:, b, :], AB[:, 1, c, :], ALU.add).then_inc(ready, 1)

    def pe(eng):
        for b in range(NB):
            eng.wait_ge(ready, b + 1)
            if b >= 2:
                eng.wait_ge(stored, b - 1)
            for k in range(KD):
                last = eng.transpose(tp[b % 2][:, k * P:(k + 1) * P], H[:, b, k * P:(k + 1) * P], ident[:, :])
            last.then_inc(turned, 1)

    return act, dve, pe, stored, NB


def modulation(nc, X, HY, HT, ident, io):
    NCK = LAYERS * 6 * D // 512
    UNROLL, LOADS = 6, 3

    def body(sb, ps, sem):
        condT = sb("condT", [P, KD, 2])
        sgm = sb("sgm", [P, KD, 2])
        w01 = sb("wmod", [P, 2, KD * 512])
        rows = sb("rows", [2, NCK * 512])
        w = [w01[:, 0, :], w01[:, 1, :], HT[:, :, :].rearrange("p k t -> p (k t)")[:, 0:KD * 512]]
        gains = HY[0:2, 0:2 * LAYERS, :].rearrange("c (n l) d -> c n l d", n=2)
        cond_hi = sb("cond_hi", [P, KD, 2], F32R)
        cond_lo = sb("cond_lo", [P, KD, 2], F32R)
        w_hi = sb("w_hi", [P, 2, KD * 512], F32R)
        w_lo = sb("w_lo", [P, 2, KD * 512], F32R)
        out = [ps(f"modp{i}", 512) for i in range(2)]
        x_in, cond_in, small_in = sem("x_in"), sem("cond_in"), sem("small_in")
        w_in = [sem(f"wmod_in{i}") for i in range(LOADS)]
        sg_done, silu_done, cond_split = sem("sg_done"), sem("silu_done"), sem("cond_split")
        hi_done, lo_done = sem("hi_done"), sem("lo_done")
        chunk_done, chunk_read = sem("chunk_done"), sem("chunk_read")
        gained, rows_out, ident0, ident1 = sem("gained"), sem("rows_out"), sem("ident0"), sem("ident1")

        with nc.Block() as block:
            @block.sync
            def _(sp):
                with sp.Fori(0, NCK // UNROLL) as i:
                    for s in range(UNROLL):
                        sp.wait_ge(lo_done, i * UNROLL + s + 1)
                        sp.dma_start(w[s % LOADS], io["w_mod"][bass.ds(i * UNROLL + s, 1), :, :].rearrange("a p n -> (a p) n"))\
                          .then_inc(w_in[s % LOADS], 16)
                sp.wait_ge(gained, 2 * LAYERS)
                sp.dma_start(io["mod_rows"].rearrange("(c n) -> c n", c=2), rows[:, :]).then_inc(rows_out, 16)
                sp.wait_ge(rows_out, 16)

            @block.scalar
            def _(act):
                act.dma_start(condT[:, :, :], io["condT"]).then_inc(cond_in, 16)
                act.dma_start(X[:, 0:SB, :], io["x_sample"].rearrange("o (b p) d -> (o p) b d", p=P)).then_inc(x_in, 16)
                act.dma_start(X[:, SB, :], io["x_prompt"].rearrange("o p d -> (o p) d")).then_inc(x_in, 16)
                act.dma_start(rows[:, :], io["b_mod"].rearrange("l n -> (l n)").unsqueeze(0).broadcast_to([2, NCK * 512])).then_inc(small_in, 16)
                for n, name in enumerate(("norm1_g", "norm2_g")):
                    act.dma_start(gains[:, n, :, :].rearrange("p l d -> p (l d)"),
                                  io[name].rearrange("l d -> (l d)").unsqueeze(0).broadcast_to([2, LAYERS * D])).then_inc(small_in, 16)
                act.wait_ge(cond_in, 16)
                act.activation(sgm[:, :, :], condT[:, :, :], ACT.Sigmoid).then_inc(sg_done, 1)
                with act.Fori(0, NCK // UNROLL) as i:
                    for s in range(UNROLL):
                        act.wait_ge(w_in[s % LOADS], i * (UNROLL // LOADS * 16) + (s // LOADS + 1) * 16)
                        act.wait_ge(chunk_done, i * UNROLL + s + 1)
                        act.activation(w_hi[:, s % 2, :], w[s % LOADS], ACT.Copy).then_inc(hi_done, 1)
                act.wait_ge(x_in, 32)

            @block.gpsimd
            def _(pool):
                pool.memset(ident[:, :], 0.0).then_inc(ident0, 1)
                pool.wait_ge(ident0, 1)
                pool.affine_select(out=ident[:, :], in_=ident[:, :], compare_op=ALU.not_equal, fill=1.0,
                                   base=0, pattern=[[-1, P]], channel_multiplier=1).then_inc(ident1, 1)
                pool.wait_ge(ident1, 1)

            @block.vector
            def _(dve):
                dve.sem_inc(chunk_read, 2)
                dve.sem_inc(lo_done, LOADS)
                dve.wait_ge(sg_done, 1)
                dve.tensor_tensor(condT[:, :, :], condT[:, :, :], sgm[:, :, :], ALU.mult).then_inc(silu_done, 1)
                dve.wait_ge(silu_done, 1)
                dve.tensor_copy(cond_hi[:, :, :], condT[:, :, :]).then_inc(cond_split, 1)
                dve.wait_ge(cond_split, 1)
                dve.tensor_tensor(cond_lo[:, :, :], condT[:, :, :], cond_hi[:, :, :].bitcast(F32),
                                  ALU.subtract).then_inc(cond_split, 1)

                def low_part(i, s):
                    dve.wait_ge(w_in[s % LOADS], i * (UNROLL // LOADS * 16) + (s // LOADS + 1) * 16)
                    dve.wait_ge(hi_done, i * UNROLL + s + 1)
                    dve.wait_ge(chunk_done, i * UNROLL + s + 1)
                    dve.tensor_tensor(w_lo[:, s % 2, :], w[s % LOADS], w_hi[:, s % 2, :].bitcast(F32),
                                      ALU.subtract).then_inc(lo_done, 1)

                def add_bias(i, s):
                    dve.wait_ge(chunk_done, i * UNROLL + s + 3)
                    cols = bass.ds(i * (UNROLL * 512) + s * 512, 512)
                    dve.tensor_tensor(rows[:, cols], out[s % 2][0:2, :], rows[:, cols], ALU.add).then_inc(chunk_read, 1)

                low_part(0, 0)
                dve.wait_ge(small_in, 48)

                def chunks(i, last):
                    for s in range(UNROLL):
                        if s + 1 < UNROLL:
                            low_part(i, s + 1)
                        elif not last:
                            low_part(i + 1, 0)
                        add_bias(i, s)

                with dve.Fori(0, NCK // UNROLL - 1) as i:
                    chunks(i, False)
                chunks(NCK // UNROLL - 1, True)
                dve.wait_ge(chunk_read, NCK + 2)
                for layer in range(LAYERS):
                    for n in range(2):
                        lo = layer * 6 * D + (3 * n + 1) * D
                        dve.scalar_tensor_tensor(out=rows[:, lo:lo + D], in0=rows[:, lo:lo + D], scalar=1.0,
                                                 in1=gains[:, n, layer, :], op0=ALU.add, op1=ALU.mult).then_inc(gained, 1)

            @block.tensor
            def _(pe):
                pe.sem_inc(chunk_done, 2)
                pe.wait_ge(cond_split, 2)
                with pe.Fori(0, NCK // UNROLL) as i:
                    for s in range(UNROLL):
                        pe.wait_ge(hi_done, i * UNROLL + s + 1)
                        pe.wait_ge(chunk_read, i * UNROLL + s + 1)
                        for k in range(KD):
                            for part in (cond_hi, cond_lo):
                                pe.matmul(out[s % 2][0:2, :], part[:, k, :], w_hi[:, s % 2, k * 512:(k + 1) * 512],
                                          start=(k == 0 and part is cond_hi), stop=False)
                        pe.wait_ge(lo_done, i * UNROLL + (s + LOADS + 1))
                        for k in range(KD):
                            last = pe.matmul(out[s % 2][0:2, :], cond_hi[:, k, :], w_lo[:, s % 2, k * 512:(k + 1) * 512],
                                             start=False, stop=(k == KD - 1))
                        last.then_inc(chunk_done, 1)

    phase(nc, "mod", body)


def load_mod(eng, io, dst, layer, section, landed):
    for c in range(2):
        lo = c * LAYERS * 6 * D + layer * 6 * D + section * D
        eng.dma_start(dst[:, c, :], broadcast_rows(io["mod_rows"], lo, D)).then_inc(landed, 16)


def project_and_peer(nc, X, H, HT, ident, iota16, layer, io):
    final = layer == LAYERS - 1

    def body(sb, ps, sem):
        pre = f"p{layer}_"
        G2 = sb("G2", [P, 2, D])
        ring = sb("ring", [P, SLOTS, 2 * D])
        FREE, NORM = 2, 6
        w_out = ring[:, FREE:NORM, :].rearrange("p s (k n) -> p (s k) n", n=D)
        AB = ring[:, NORM:NORM + 2, :].rearrange("p s (c d) -> p s c d", c=2)
        G1 = ring[:, NORM + 2, :].rearrange("p (c d) -> p c d", c=2)
        squares = ring[:, NORM + 3, 0:D]
        ss, rt, rs = (sb(n, [P, 2 * NB]) for n in ("ss", "rt", "rs"))
        if final:
            final_g = sb("final_g", [P, D])
        else:
            nextAB = sb("nextAB", [P, 2, 2, D])
        wq = sb("wq", [P, KD, 2 * P])
        keys = sb("keys", [P, 2, P])
        qT = sb("qT", [P, 2, T])
        qN = sb("qN", [P, 2, T])
        best = sb("best", [P, 2, TOPK])
        besti = sb("besti", [P, 2, TOPK], U32)
        bestf = sb("bestf", [P, 2, TOPK])
        work = sb("work", [P, 2, NK])
        cand = sb("cand", [P, TOPK * TOPK])
        candw = sb("candw", [P, TOPK * TOPK])
        top = sb("top", [P, TOPK])
        negtop = sb("negtop", [P, 1])
        topi = sb("topi", [P, TOPK], U32)
        pab = sb("pab", [P, 2, TOPK], U32)
        onehot = sb("onehot", [P, 2, TOPK, TOPK])
        pick = sb("pick", [P, 2, TOPK])
        index = sb("index", [P, PER_HEAD], U32)
        expo = sb("expo", [P, TOPK])
        total = sb("total", [P, 1])
        inv = sb("inv", [P, 1])
        gate = sb("gate", [P, PER_HEAD])
        dots = sb("dots", [P, PER_HEAD])
        acts = sb("acts", [P, PER_HEAD])
        diag = sb("diag", [P, NDIAG, P])
        tmp = sb("tmp", [P, D])
        acc = [ps(f"acc{i}", 1024) for i in range(2)]
        qp = ps("qp", 1024)
        sc = ps("sc", 512)
        q0 = ps("q0", 512)

        mod_in, g2_in = sem(pre + "mod_in"), sem(pre + "g2_in")
        w_in = [sem(pre + f"w_in{i}") for i in range(KD // 2)]
        g1_in, projected, gated, x_ready = (sem(pre + n) for n in ("g1_in", "projected", "gated", "x_ready"))
        squared, shifted, rooted, inverted = (sem(pre + n) for n in ("squared", "shifted", "rooted", "inverted"))
        scaled, h_ready, turned, h_stored = (sem(pre + n) for n in ("scaled", "h_ready", "turned", "h_stored"))
        q0_done, q0_stored = sem(pre + "q0_done"), sem(pre + "q0_stored")
        next_in, y_out = sem(pre + "next_in"), sem(pre + "y_out")
        landed = [sem(pre + f"landed{i}") for i in range(SLOTS)]
        slot_free = sem(pre + "slot_free")
        index_ready = sem(pre + "index_ready")
        dot_done, act_done, diag_done = sem(pre + "dot_done"), sem(pre + "act_done"), sem(pre + "diag_done")
        added = sem(pre + "added")
        wq_in, keys_in = sem(pre + "wq_in"), sem(pre + "keys_in")
        q_done, q_stored, qt_ready = sem(pre + "q_done"), sem(pre + "q_stored"), sem(pre + "qt_ready")
        sc_done, sc_used = sem(pre + "sc_done"), sem(pre + "sc_used")
        top_ready, exp_done, rstep = sem(pre + "top_ready"), sem(pre + "exp_done"), sem(pre + "rstep")
        tmp_done = sem(pre + "tmp_done")
        RSTEPS = 26
        w_q, kT, uv = io["w_q"], io["keysT"], io["uv"]

        def heads(eng, body_of_head):
            with eng.Fori(0, HEADS - 1) as h:
                body_of_head(h, False)
            body_of_head(HEADS - 1, True)

        def next_unit(b, last):
            return None if last and b == NB - 1 else (b + 1) % NB

        with nc.Block() as block:
            @block.sync
            def _(sp):
                for i in range(KD // 2):
                    sp.dma_start(w_out[:, 2 * i:2 * i + 2, :],
                                 io["w_out"][layer, 2 * i * P:(2 * i + 2) * P, :].rearrange("(k p) n -> p k n", p=P))\
                        .then_inc(w_in[i], 16)
                load_mod(sp, io, G1, layer, 2, g1_in)
                load_mod(sp, io, AB[:, 0, :, :], layer, 4, mod_in)
                load_mod(sp, io, AB[:, 1, :, :], layer, 3, mod_in)
                sp.dma_start(wq[:, :, :].rearrange("p k n -> p (k n)"), w_q[layer * HEADS, :, :]).then_inc(wq_in, 16)
                sp.dma_start(keys[:, :, :].rearrange("p a n -> p (a n)"), kT[layer * HEADS, :, :]).then_inc(keys_in, 16)
                load_mod(sp, io, G2, layer, 5, g2_in)
                if final:
                    sp.dma_start(final_g[:, :], broadcast_rows(io["final_g"], 0, D)).then_inc(next_in, 16)
                else:
                    load_mod(sp, io, nextAB[:, 0, :, :], layer + 1, 1, next_in)
                    load_mod(sp, io, nextAB[:, 1, :, :], layer + 1, 0, next_in)
                with sp.Fori(0, HEADS - 1) as h:
                    sp.wait_ge(q_done, h * 2 + 2)
                    sp.dma_start(wq[:, :, :].rearrange("p k n -> p (k n)"),
                                 w_q[bass.ds(h + (layer * HEADS + 1), 1), :, :].rearrange("a p n -> (a p) n")).then_inc(wq_in, 16)
                    sp.wait_ge(sc_done, h * NB + NB)
                    sp.dma_start(keys[:, :, :].rearrange("p a n -> p (a n)"),
                                 kT[bass.ds(h + (layer * HEADS + 1), 1), :, :].rearrange("a p n -> (a p) n")).then_inc(keys_in, 16)
                sp.wait_ge(g2_in, 32)
                if final:
                    for b in range(NB):
                        sp.wait_ge(h_ready, NB + b + 1)
                        dst = io["y_sample"][0, b * P:(b + 1) * P, :] if b < SB else io["y_prompt"][0, :, :]
                        sp.dma_start(dst, H[:, b, :]).then_inc(y_out, 16)
                    sp.wait_ge(y_out, 16 * NB)

            @block.gpsimd
            def _(pool):
                def head(h, last):
                    for j in range(PER_HEAD):
                        if j == FREE:
                            pool.wait_ge(projected, NB)
                        if j == NORM:
                            pool.wait_ge(h_ready, NB)
                        if j % TOPK == 0:
                            pool.wait_ge(index_ready, h * NB + (j // TOPK + 1))
                        wait_apart(pool, slot_free, h * PER_HEAD + (j + 1))
                        pool.indirect_dma_start(ring[:, j % SLOTS, :], None, uv[:, :],
                                                bass.IndirectOffsetOnAxis(ap=index[:, j:j + 1], axis=0),
                                                element_offset=layer * EXPERTS * 2 * D)\
                            .then_inc(landed[j % SLOTS], 16)

                heads(pool, head)

            @block.scalar
            def _(act):
                def root_mean_square(n, squares):
                    b = n % NB
                    act.activation(squares, X[:, b, :], ACT.Square, accum_out=ss[:, n:n + 1]).then_inc(squared, 1)
                    act.wait_ge(squared, n + 1)
                    act.activation(rt[:, n:n + 1], ss[:, n:n + 1], ACT.Copy, scale=1.0 / D, bias=EPS).then_inc(shifted, 1)
                    act.wait_ge(shifted, n + 1)
                    act.activation(rt[:, n:n + 1], rt[:, n:n + 1], ACT.Sqrt).then_inc(rooted, 1)

                def store_turned(n):
                    b = n % NB
                    act.wait_ge(turned, n + 1)
                    act.activation(HT[:, :, b * P:(b + 1) * P], qp[:, :].rearrange("p (k t) -> p k t", k=KD),
                                   ACT.Copy).then_inc(h_stored, 1)

                def store_q0(b):
                    act.wait_ge(q0_done, b + 1)
                    act.activation(qT[:, :, b * P:(b + 1) * P], q0[:, 0:2 * P].rearrange("p (a t) -> p a t", a=2),
                                   ACT.Copy).then_inc(q0_stored, 1)

                for b in range(NB):
                    act.wait_ge(x_ready, b + 1)
                    root_mean_square(b, squares)
                    if b == 1:
                        store_turned(0)
                    if b == 2:
                        store_q0(0)
                for b in range(1, NB):
                    store_turned(b)
                    if b >= 2:
                        store_q0(b - 1)
                store_q0(NB - 1)
                act.wait_ge(q0_stored, NB)
                act.sem_inc(q_stored, 2)
                act.sem_inc(qt_ready, 1)

                def exponent(unit):
                    act.wait_ge(top_ready, unit + 1)
                    act.activation(expo[:, :], top[:, :], ACT.Exp, bias=negtop[:, 0:1],
                                   accum_out=total[:, 0:1]).then_inc(exp_done, 1)

                def store_q(h, half):
                    act.wait_ge(q_done, h * 2 + (half + 1))
                    act.activation(qN[:, half, :], qp[:, 0:T], ACT.Copy).then_inc(q_stored, 1)

                def next_norm(b):
                    act.wait_ge(added, (HEADS - 1) * NB + b + 2)
                    root_mean_square(NB + b, qN[:, :, :].rearrange("p a t -> p (a t)")[:, 0:D])

                def hand_q(h):
                    act.wait_ge(q_stored, h * 2 + 2)
                    act.activation(qT[:, :, :], qN[:, :, :], ACT.Copy).then_inc(qt_ready, 1)

                exponent(0)

                def head(h, last):
                    for j in range(PER_HEAD):
                        b, s = divmod(j, TOPK)
                        act.wait_ge(dot_done, h * PER_HEAD + (j + 1))
                        act.activation(acts[:, j:j + 1], dots[:, j:j + 1], ACT.Gelu_apprx_tanh).then_inc(act_done, 1)
                        if s == 5 and next_unit(b, last) is not None:
                            exponent(h * NB + (b + 1))
                        if not last and j == 28:
                            store_q(h + 1, 0)
                        if not last and j == 52:
                            store_q(h + 1, 1)
                        if not last and j == 56:
                            act.wait_ge(sc_done, h * NB + NB)
                            hand_q(h + 1)
                        if last and b and s == 9:
                            next_norm(b - 1)
                        if last and not final and b and s == 15:
                            store_turned(NB + b - 1)
                    if last:
                        next_norm(NB - 1)
                        if not final:
                            store_turned(2 * NB - 1)

                heads(act, head)

            @block.vector
            def _(dve):
                dve.sem_inc(added, 1)

                def residual(b):
                    dve.wait_ge(projected, b + 1)
                    dve.tensor_tensor(tmp[:, :], acc[b % 2][:, :], G1[:, cond_of(b), :], ALU.mult).then_inc(gated, 1)
                    dve.wait_ge(gated, b + 1)
                    dve.tensor_tensor(X[:, b, :], X[:, b, :], tmp[:, :], ALU.add).then_inc(x_ready, 1)

                def norm(n):
                    b, c = n % NB, cond_of(n % NB)
                    dve.wait_ge(rooted, n + 1)
                    dve.reciprocal(rs[:, n:n + 1], rt[:, n:n + 1]).then_inc(inverted, 1)
                    dve.wait_ge(inverted, n + 1)
                    if n >= NB and final:
                        dve.scalar_tensor_tensor(out=H[:, b, :], in0=X[:, b, :], scalar=rs[:, n:n + 1],
                                                 in1=final_g[:, :], op0=ALU.mult, op1=ALU.mult).then_inc(h_ready, 1)
                        return
                    gain_shift = nextAB if n >= NB else AB
                    dve.scalar_tensor_tensor(out=H[:, b, :], in0=X[:, b, :], scalar=rs[:, n:n + 1],
                                             in1=gain_shift[:, 0, c, :], op0=ALU.mult, op1=ALU.mult).then_inc(scaled, 1)
                    dve.wait_ge(scaled, n + 1)
                    dve.tensor_tensor(H[:, b, :], H[:, b, :], gain_shift[:, 1, c, :], ALU.add).then_inc(h_ready, 1)

                def route_a(unit):
                    r = Count(dve, rstep, unit * RSTEPS, apart=True)
                    halves = [sc[:, 0:NK], sc[:, NK:2 * NK]]
                    wait_apart(dve, sc_done, unit + 1)
                    for a in range(2):
                        r.add(dve.max(best[:, a, 0:8], halves[a]))
                    r.wait()
                    for a in range(2):
                        r.add(dve.match_replace(work[:, a, :], best[:, a, 0:8], halves[a], -3e38))
                    r.wait()
                    for a in range(2):
                        r.add(dve.max(best[:, a, 8:16], work[:, a, :]))
                    for a in range(2):
                        r.add(dve.max_index(besti[:, a, 0:8], best[:, a, 0:8], halves[a]))
                    r.wait()
                    dve.sem_inc(sc_used, 1)
                    return r

                def route_b(r):
                    for a in range(2):
                        r.add(dve.max_index(besti[:, a, 8:16], best[:, a, 8:16], work[:, a, :]))
                    r.add(dve.tensor_tensor(cand[:, :].rearrange("p (a b) -> p a b", a=TOPK),
                                            best[:, 0, :].unsqueeze(2).broadcast_to([P, TOPK, TOPK]),
                                            best[:, 1, :].unsqueeze(1).broadcast_to([P, TOPK, TOPK]), ALU.add))
                    r.wait()
                    r.add(dve.tensor_scalar(bestf[:, 0, :], besti[:, 0, :], float(NK), None, ALU.mult))
                    r.add(dve.tensor_copy(bestf[:, 1, :], besti[:, 1, :]))
                    r.add(dve.max(top[:, 0:8], cand[:, :]))
                    r.wait()
                    r.add(dve.match_replace(candw[:, :], top[:, 0:8], cand[:, :], -3e38))
                    r.add(dve.tensor_scalar(negtop[:, :], top[:, 0:1], -1.0, None, ALU.mult))
                    r.add(dve.max_index(topi[:, 0:8], top[:, 0:8], cand[:, :]))
                    r.wait()

                def route_c(r, b):
                    r.add(dve.max(top[:, 8:16], candw[:, :]))
                    r.wait()
                    dve.sem_inc(top_ready, 1)
                    r.add(dve.max_index(topi[:, 8:16], top[:, 8:16], candw[:, :]))
                    r.wait()
                    r.add(dve.tensor_scalar(pab[:, 0, :], topi[:, :], 4, None, ALU.logical_shift_right))
                    r.add(dve.tensor_scalar(pab[:, 1, :], topi[:, :], TOPK - 1, None, ALU.bitwise_and))
                    r.wait()
                    r.add(dve.tensor_tensor(onehot[:, :, :, :].rearrange("p a k r -> p (a k) r"),
                                            pab[:, :, :].rearrange("p a k -> p (a k)").unsqueeze(2).broadcast_to([P, 2 * TOPK, TOPK]),
                                            iota16[:, :].unsqueeze(1).broadcast_to([P, 2 * TOPK, TOPK]), ALU.is_equal))
                    r.wait()
                    r.add(dve.tensor_tensor(onehot[:, :, :, :], onehot[:, :, :, :],
                                            bestf[:, :, :].unsqueeze(2).broadcast_to([P, 2, TOPK, TOPK]), ALU.mult))
                    r.wait()
                    r.add(dve.tensor_reduce(pick[:, :, :].rearrange("p a k -> p (a k)"),
                                            onehot[:, :, :, :].rearrange("p a k r -> p (a k) r"), AX.X, ALU.add))
                    r.wait()
                    dve.tensor_tensor(index[:, b * TOPK:(b + 1) * TOPK], pick[:, 0, :], pick[:, 1, :],
                                      ALU.add).then_inc(index_ready, 1)

                def route_d(r, unit, b):
                    dve.wait_ge(exp_done, unit + 1)
                    r.add(dve.reciprocal(inv[:, :], total[:, :]))
                    r.wait()
                    r.add(dve.tensor_scalar(gate[:, b * TOPK:(b + 1) * TOPK], expo[:, :], inv[:, 0:1], None, ALU.mult))
                    r.wait()
                    assert r.n == RSTEPS, r.n

                dve.wait_ge(g1_in, 32)
                dve.wait_ge(mod_in, 64)
                for b in range(NB):
                    residual(b)
                    norm(b)
                    if b == 2:
                        r = route_a(0)
                        route_b(r)
                    if b == 3:
                        route_c(r, 0)
                route_d(r, 0, 0)
                dve.wait_ge(g2_in, 32)
                dve.wait_ge(next_in, 16 if final else 64)

                def dot(h, j):
                    dve.wait_ge(landed[j % SLOTS], (h * (PER_HEAD // SLOTS) + (j // SLOTS + 1)) * 16)
                    u = ring[:, j % SLOTS, 0:D]
                    dve.tensor_tensor_reduce(u, u, H[:, j // TOPK, :], 1.0, 0.0, ALU.mult, ALU.add,
                                             dots[:, j:j + 1]).then_inc(dot_done, 1)

                def weight(h, j):
                    dve.wait_ge(act_done, h * PER_HEAD + (j + 1))
                    dve.wait_ge(slot_free, h * PER_HEAD + (j + 1 + SLOTS - NDIAG))
                    dve.tensor_scalar(diag[:, j % NDIAG, :], ident[:, :], acts[:, j:j + 1], gate[:, j:j + 1],
                                      ALU.mult, ALU.mult).then_inc(diag_done, 1)

                def add_unit(h, b):
                    dve.wait_ge(slot_free, h * PER_HEAD + ((b + 1) * TOPK + SLOTS))
                    dve.tensor_tensor(tmp[:, :], acc[b % 2][:, :], G2[:, cond_of(b), :], ALU.mult).then_inc(tmp_done, 1)
                    dve.wait_ge(tmp_done, h * NB + (b + 1))
                    dve.tensor_tensor(X[:, b, :], X[:, b, :], tmp[:, :], ALU.add).then_inc(added, 1)

                def head(h, last):
                    r = None
                    for j in range(PER_HEAD):
                        b, s = divmod(j, TOPK)
                        dot(h, j)
                        if j:
                            weight(h, j - 1)
                        nb = next_unit(b, last)
                        unit = h * NB + (b + 1)
                        if nb is not None:
                            if s == 1:
                                r = route_a(unit)
                            if s == 3:
                                route_b(r)
                            if s == 5:
                                route_c(r, nb)
                            if s == 7:
                                route_d(r, unit, nb)
                        if s == 7 and b:
                            add_unit(h, b - 1)
                        if last and s == 12 and b:
                            norm(NB + b - 1)
                    weight(h, PER_HEAD - 1)
                    add_unit(h, NB - 1)
                    if last:
                        norm(2 * NB - 1)

                heads(dve, head)

            @block.tensor
            def _(pe):
                pe.sem_inc(slot_free, SLOTS)

                def project(b):
                    if b >= 2:
                        pe.wait_ge(gated, b - 1)
                    for k in range(KD):
                        if b == 0 and k % 2 == 0:
                            pe.wait_ge(w_in[k // 2], 16)
                        for lo in (0, 512):
                            last = pe.matmul(acc[b % 2][:, lo:lo + 512], H[:, b, k * P:(k + 1) * P],
                                             w_out[:, k, lo:lo + 512], start=(k == 0), stop=(k == KD - 1))
                    last.then_inc(projected, 1)

                def turn(n):
                    b = n % NB
                    pe.wait_ge(h_ready, n + 1)
                    if n:
                        pe.wait_ge(h_stored, n)
                    for k in range(KD):
                        last = pe.transpose(qp[:, k * P:(k + 1) * P], H[:, b, k * P:(k + 1) * P], ident[:, :])
                    last.then_inc(turned, 1)

                def first_query(b):
                    pe.wait_ge(h_stored, b + 1)
                    if b:
                        pe.wait_ge(q0_stored, b)
                    else:
                        pe.wait_ge(wq_in, 16)
                    for a in range(2):
                        for k in range(KD):
                            last = pe.matmul(q0[:, a * P:(a + 1) * P], wq[:, k, a * P:(a + 1) * P],
                                             HT[:, k, b * P:(b + 1) * P], start=(k == 0), stop=(k == KD - 1))
                    last.then_inc(q0_done, 1)

                def query(h, n):
                    half, k = divmod(n, KD)
                    if n == 0:
                        pe.wait_ge(wq_in, h * 16 + 16)
                    if k == 0:
                        pe.wait_ge(q_stored, h * 2 + half)
                    for lo, hi in ((0, LS), (LS, T)):
                        last = pe.matmul(qp[:, lo:hi], wq[:, k, half * P:(half + 1) * P], HT[:, k, lo:hi],
                                         start=(k == 0), stop=(k == KD - 1), skip_group_check=True)
                    if k == KD - 1:
                        last.then_inc(q_done, 1)

                def scores(h, b, unit):
                    if unit is None:
                        pe.wait_ge(q0_stored, 1)
                        pe.wait_ge(keys_in, 16)
                    else:
                        pe.wait_ge(qt_ready, h + 1)
                        pe.wait_ge(keys_in, h * 16 + 16)
                        pe.wait_ge(sc_used, unit)
                    for a in range(2):
                        last = pe.matmul(sc[:, a * NK:(a + 1) * NK], qT[:, a, b * P:(b + 1) * P], keys[:, a, :],
                                         start=True, stop=True)
                    last.then_inc(sc_done, 1)

                for b in range(NB):
                    project(b)
                    if b == 1:
                        turn(0)
                    if b == 2:
                        first_query(0)
                        scores(0, 0, None)
                for b in range(1, NB):
                    turn(b)
                    if b >= 2:
                        first_query(b - 1)
                first_query(NB - 1)
                pe.wait_ge(q0_done, NB)
                pe.sem_inc(q_done, 2)

                def head(h, last):
                    for b in range(NB):
                        nb = next_unit(b, last)
                        if nb is not None:
                            scores(h + 1 if nb == 0 else h, nb, h * NB + (b + 1))
                        pe.wait_ge(added, h * NB + (1 if b == 0 else b))
                        for e in range(TOPK):
                            j = b * TOPK + e
                            pe.wait_ge(diag_done, h * PER_HEAD + (j + 1))
                            for lo in (0, 512):
                                last_mm = pe.matmul(acc[b % 2][:, lo:lo + 512], diag[:, j % NDIAG, :],
                                                    ring[:, j % SLOTS, D + lo:D + lo + 512],
                                                    start=(e == 0), stop=(e == TOPK - 1))
                            last_mm.then_inc(slot_free, 1)
                            if not last and j % 3 == 2 and j // 3 < 2 * KD:
                                query(h + 1, j // 3)
                            if last and not final and b and e == 14:
                                if b == 1:
                                    pe.wait_ge(q_stored, 2 * HEADS)
                                turn(NB + b - 1)
                    if last and not final:
                        turn(2 * NB - 1)

                heads(pe, head)

    phase(nc, f"peer{layer}", body)


def hgrn(nc, X, HT, YT, watt, ident, io):
    def body(sb, ps, sem):
        wfb = sb("wfb", [P, KD, 2 * P])
        wqvg = sb("wqvg", [P, KD, 3 * P])
        lbr = sb("lbr", [P, 2, 2, HG])
        lbx = sb("lbx", [P, 2, HG])
        lbe = sb("lbe", [P, 2, 2, HG])
        lb = sb("lb", [P, 2, HG])
        oml = sb("oml", [P, 2, HG])
        gn = sb("gn", [P, HG])
        reset = sb("reset", [P, T])
        tri = sb("tri", [P, 2, P])
        AB = sb("ABe", [P, 2, 2, D])
        work = lambda n: sb(n, [P, T])
        Q, SQ = work("Q"), work("SQ")
        V = sb("V", [P, NB, P])
        Vm = sb("Vm", [P, NB, 2, P])
        ZG = sb("ZG", [P, NB, P])
        ON = sb("ON", [P, NB, P])
        K = [work("Kf"), work("Kb")]
        G = [work("Gf"), work("Gb")]
        B = [work("Bf"), work("Bb")]
        QI = [work("QIf"), work("QIb")]
        KI = [work("KIf"), work("KIb")]
        QB = [work("QBf"), work("QBb")]
        KL = [work("KLf"), work("KLb")]
        KLT = [work("KLTf"), work("KLTb")]
        AT = [work("ATf"), work("ATb")]
        EBL = sb("EBL", [P, 2, NCH])
        S = [sb("Sf", [P, NCH + 1, P]), sb("Sb", [P, NCH + 1, P])]
        SS = sb("SS", [P, NB])
        RT = sb("RT", [P, NB])
        RS = sb("RS", [P, NB])
        D0, D1, D2, D3 = (ps(f"D{i}", 1024) for i in range(4))

        mod_in, lb_in, gn_in, watt_in = sem("e_mod_in"), sem("lb_in"), sem("gn_in"), sem("watt_in")
        n_act, n_dve, n_pe, h_stored, n_stored = norm_parts(sb, sem, "e_", X, YT, HT, ident, AB, mod_in, 64, D2[:, :], [D0, D1])
        consts, czero = sem("consts"), sem("czero")
        lb_step, lb_exp, lb_ready = sem("lb_step"), sem("lb_exp"), sem("lb_ready")
        wfb_in, wqvg_in, s0_in, st_out = (sem(n) for n in ("wfb_in", "wqvg_in", "s0_in", "st_out"))
        proj = [sem(f"proj_{n}") for n in "fbqv"]
        sig_done, q_made, ln_done, diff_done, exp_done = (sem(n) for n in ("sig_done", "q_made", "ln_done", "diff_done", "e_exp"))
        v_done, zg_sig, vg_read, vm_done = (sem(n) for n in ("v_done", "zg_sig", "vg_read", "vm_done"))
        kl_done, klt_psum, klt_done = sem("kl_done"), sem("klt_psum"), sem("klt_done")
        at_psum, at_done, u_done, s_done = sem("at_psum"), sem("at_done"), sem("u_done"), sem("s_done")
        o_done, o_sq, ss_done, rt_done = sem("o_done"), sem("o_sq"), sem("ss_done"), sem("rt_done")
        on_done, on_turned, head_done, dstep = sem("on_done"), sem("on_turned"), sem("head_done"), sem("dstep")
        states_done = sem("states_done")
        st_free = sem("st_free")
        DSTEPS = 31
        NCONST = 12
        first = [0, CH - 1]
        final = [CH - 1, 0]
        middle = [CH // 2 - 1, CH // 2]

        def by_chunk(t):
            return t[:, :].rearrange("p (c t) -> p c t", t=CH)

        def at_step(t, i):
            return by_chunk(t)[:, :, i:i + 1].broadcast_to([P, NCH, CH])

        with nc.Block() as block:
            @block.sync
            def _(sp):
                load_mod(sp, io, AB[:, 0, :, :], 0, 1, mod_in)
                load_mod(sp, io, AB[:, 1, :, :], 0, 0, mod_in)
                sp.dma_start(lbr[:, :, :, :], io["hgrn_lb"]).then_inc(lb_in, 16)
                sp.dma_start(gn[:, :], io["gnormT"]).then_inc(gn_in, 16)
                sp.sem_inc(st_free, 1)

                def weights(tile, name, h, landed):
                    sp.dma_start(tile[:, :, :].rearrange("p k n -> p (k n)"),
                                 io[name][bass.ds(h, 1), :, :].rearrange("a p n -> (a p) n")).then_inc(landed, 16)

                def first_states(h):
                    sp.dma_start(S[0][:, 0, :], io["state0"][0, bass.ds(h, 1), :, :].rearrange("a p n -> (a p) n")).then_inc(s0_in, 16)
                    sp.dma_start(S[1][:, SCH - 1, :], io["state0"][1, bass.ds(h, 1), :, :].rearrange("a p n -> (a p) n")).then_inc(s0_in, 16)

                def head(h, last):
                    if not last:
                        sp.wait_ge(proj[1], h + 1)
                        weights(wfb, "w_hgrn_fb", h + 1, wfb_in)
                        sp.wait_ge(proj[3], h + 2)
                        weights(wqvg, "w_hgrn_qvg", h + 1, wqvg_in)
                    sp.wait_ge(s_done, h * 2 + 2)
                    sp.dma_start(io["new_hf"][0, 0, bass.ds(h, 1), :, :].rearrange("a p n -> (a p) n"), S[0][:, NCH, :]).then_inc(st_out, 16)
                    sp.dma_start(io["new_hb"][0, 0, bass.ds(h, 1), :, :].rearrange("a p n -> (a p) n"), S[1][:, NCH, :]).then_inc(st_out, 16)
                    sp.wait_ge(st_out, h * 32 + 32)
                    sp.sem_inc(st_free, 1)
                    if not last:
                        sp.wait_ge(head_done, h + 2)
                        first_states(h + 1)

                weights(wfb, "w_hgrn_fb", 0, wfb_in)
                weights(wqvg, "w_hgrn_qvg", 0, wqvg_in)
                first_states(0)
                with sp.Fori(0, HG - 1) as h:
                    head(h, False)
                head(HG - 1, True)
                sp.dma_start(watt[:, :, :].rearrange("p k n -> p (k n)"), io["w_att"]).then_inc(watt_in, 16)
                sp.wait_ge(st_out, 32 * HG)
                sp.wait_ge(watt_in, 16)

            @block.gpsimd
            def _(pool):
                c = Count(pool, consts)
                c.add(pool.memset(reset[:, :], 1.0))
                c.add(pool.memset(tri[:, :, :], 1.0))
                c.add(pool.memset(Vm[:, :, :, :], 0.0))
                for d in range(2):
                    c.add(pool.memset(AT[d][:, :], 0.0))
                    c.add(pool.memset(S[d][:, SCH + d * (NCH - SCH - 1), :], 0.0))
                c.wait()
                c.add(pool.memset(by_chunk(reset)[:, :, 0:1], 0.0))
                c.add(pool.affine_select(out=tri[:, 0, :], in_=tri[:, 0, :], compare_op=ALU.is_ge, fill=0.0,
                                         base=0, pattern=[[1, P]], channel_multiplier=-1))
                c.add(pool.affine_select(out=tri[:, 1, :], in_=tri[:, 1, :], compare_op=ALU.is_ge, fill=0.0,
                                         base=0, pattern=[[-1, P]], channel_multiplier=1))
                c.wait()
                c.add(pool.affine_select(out=tri[:, 0, CH:P], in_=tri[:, 0, CH:P], compare_op=ALU.is_ge, fill=0.0,
                                         base=-CH, pattern=[[0, CH]], channel_multiplier=1))
                c.add(pool.affine_select(out=tri[:, 1, 0:CH], in_=tri[:, 1, 0:CH], compare_op=ALU.is_ge, fill=0.0,
                                         base=CH - 1, pattern=[[0, CH]], channel_multiplier=-1))
                assert c.n == NCONST
                with pool.Fori(0, HG) as h:
                    pool.wait_ge(v_done, h * 2 + 2)
                    wait_apart(pool, u_done, h * 2 + 1)
                    for half in range(2):
                        rows = slice(half * CH, half * CH + CH)
                        pool.tensor_copy(Vm[rows, :, half, :], V[rows, :, :]).then_inc(vm_done, 1)

            @block.scalar
            def _(act):
                act.wait_ge(lb_step, 2)
                act.activation(lbe[:, :, :, :], lbe[:, :, :, :], ACT.Exp).then_inc(lb_exp, 1)
                n_act(act)
                act.wait_ge(lb_ready, 1)
                with act.Fori(0, HG) as h:
                    act.wait_ge(head_done, h + 1)
                    for d, (src, p) in enumerate(((D0, proj[0]), (D1, proj[1]))):
                        act.wait_ge(p, h + 1)
                        act.activation(G[d][:, :], src[:, 0:T], ACT.Sigmoid)
                        act.activation(K[d][:, :], src[:, 0:T], ACT.Sigmoid, scale=-1.0).then_inc(sig_done, 1)
                    act.wait_ge(proj[2], h + 1)
                    act.activation(SQ[:, :], D0[:, 0:T], ACT.Sigmoid).then_inc(sig_done, 1)
                    act.wait_ge(sig_done, h * 3 + 3)
                    for d in range(2):
                        act.activation(G[d][:, :], G[d][:, :], ACT.Ln, scale=oml[:, d, bass.ds(h, 1)],
                                       bias=lb[:, d, bass.ds(h, 1)]).then_inc(ln_done, 1)
                    for d in range(2):
                        act.wait_ge(diff_done, h * 4 + (2 * d + 2))
                        act.activation(QI[d][:, :], G[d][:, :], ACT.Exp)
                        act.activation(KI[d][:, :], G[d][:, :], ACT.Exp, scale=-1.0)
                        act.activation(QB[d][:, :], B[d][:, :], ACT.Exp)
                        act.activation(KL[d][:, :], KL[d][:, :], ACT.Exp).then_inc(exp_done, 1)
                    act.wait_ge(proj[3], h + 2)
                    vg = D1[:, :].rearrange("p (b n) -> p b n", n=2 * P)
                    act.activation(V[:, 0:SB, :], vg[:, :, 0:P], ACT.Copy).then_inc(v_done, 1)
                    act.activation(V[:, SB, :], D0[:, T:T + P], ACT.Copy).then_inc(v_done, 1)
                    act.activation(ZG[:, 0:SB, :], vg[:, :, P:2 * P], ACT.Sigmoid)
                    act.activation(ZG[:, SB, :], D0[:, T + P:T + 2 * P], ACT.Sigmoid).then_inc(zg_sig, 1)
                    for d, src in enumerate((D2, D3)):
                        act.wait_ge(klt_psum, h * 2 + (d + 1))
                        act.activation(KLT[d][:, :], src[:, 0:T], ACT.Copy).then_inc(klt_done, 1)
                    act.wait_ge(o_done, h + 1)
                    act.activation(ON[:, :, :].rearrange("p b v -> p (b v)"), D2[:, 0:T], ACT.Square).then_inc(o_sq, 1)
                    act.wait_ge(ss_done, h + 1)
                    act.activation(RT[:, :], SS[:, :], ACT.Sqrt).then_inc(rt_done, 1)

            @block.vector
            def _(dve):
                dve.sem_inc(head_done, 1)
                c = Count(dve, lb_step)
                dve.wait_ge(lb_in, 16)
                c.add(dve.tensor_tensor(lbx[:, :, :], lbr[:, :, 0, :], lbr[:, :, 1, :], ALU.max))
                c.wait()
                c.add(dve.tensor_tensor(lbe[:, :, :, :], lbr[:, :, :, :],
                                        lbx[:, :, :].unsqueeze(2).broadcast_to([P, 2, 2, HG]), ALU.subtract))
                dve.wait_ge(lb_exp, 1)
                c.add(dve.tensor_tensor(lbx[:, :, :], lbe[:, :, 0, :], lbe[:, :, 1, :], ALU.add))
                c.wait()
                c.add(dve.reciprocal(lbx[:, :, :], lbx[:, :, :]))
                c.wait()
                c.add(dve.tensor_tensor(lb[:, :, :], lbe[:, :, 0, :], lbx[:, :, :], ALU.mult))
                c.wait()
                dve.tensor_scalar(oml[:, :, :], lb[:, :, :], -1.0, 1.0, ALU.mult, ALU.add).then_inc(lb_ready, 1)
                n_dve(dve)
                dve.wait_ge(lb_ready, 1)
                dve.wait_ge(gn_in, 16)
                dve.wait_ge(consts, NCONST)
                with dve.Fori(0, HG) as h:
                    r = Count(dve, dstep, h * DSTEPS)
                    for d in range(2):
                        dve.wait_ge(sig_done, h * 3 + (d + 1))
                        r.add(dve.tensor_scalar(K[d][:, :], K[d][:, :], oml[:, d, bass.ds(h, 1)], None, ALU.mult))
                    dve.wait_ge(sig_done, h * 3 + 3)
                    dve.tensor_tensor(Q[:, :], D0[:, 0:T], SQ[:, :], ALU.mult).then_inc(q_made, 1)
                    for d in range(2):
                        dve.wait_ge(ln_done, h * 2 + (d + 1))
                        step = slice(None, None, -1) if d else slice(None)
                        r.add(dve.tensor_tensor_scan(B[d][:, step], reset[:, :], G[d][:, step], 0.0, ALU.mult, ALU.add))
                        r.wait()
                        dve.tensor_tensor(by_chunk(G[d]), by_chunk(B[d]), at_step(B[d], middle[d]),
                                          ALU.subtract).then_inc(diff_done, 1)
                        dve.tensor_tensor(by_chunk(KL[d]), at_step(B[d], final[d]), by_chunk(B[d]),
                                          ALU.subtract).then_inc(diff_done, 1)
                    dve.wait_ge(q_made, h + 1)
                    for d in range(2):
                        dve.wait_ge(exp_done, h * 2 + (d + 1))
                        r.add(dve.tensor_copy(EBL[:, d, :], by_chunk(QB[d])[:, :, final[d]]))
                        r.wait()
                        r.add(dve.tensor_tensor(QI[d][:, :], QI[d][:, :], Q[:, :], ALU.mult))
                        r.add(dve.tensor_tensor(KI[d][:, :], KI[d][:, :], K[d][:, :], ALU.mult))
                        r.add(dve.tensor_tensor(QB[d][:, :], QB[d][:, :], Q[:, :], ALU.mult))
                        r.wait()
                        dve.tensor_tensor(KL[d][:, :], KL[d][:, :], K[d][:, :], ALU.mult).then_inc(kl_done, 1)
                    dve.wait_ge(zg_sig, h + 1)
                    vg = D1[:, :].rearrange("p (b n) -> p b n", n=2 * P)
                    dve.tensor_tensor(ZG[:, 0:SB, :], ZG[:, 0:SB, :], vg[:, :, P:2 * P], ALU.mult).then_inc(vg_read, 1)
                    dve.tensor_tensor(ZG[:, SB, :], ZG[:, SB, :], D0[:, T + P:T + 2 * P], ALU.mult).then_inc(vg_read, 1)
                    for d, src in enumerate((D2, D3)):
                        wait_apart(dve, at_psum, h * 2 + (d + 1))
                        dve.copy_predicated(AT[d][:, :].rearrange("p (b t) -> p b t", t=P),
                                            tri[:, d, :].bitcast(U32).unsqueeze(1).broadcast_to([P, NB, P]),
                                            src[:, 0:T].rearrange("p (b t) -> p b t", t=P)).then_inc(at_done, 1)
                    dve.wait_ge(s0_in, h * 32 + 32)
                    dve.wait_ge(st_free, h + 1)

                    def advance(d, src, dst, chunk):
                        if chunk < SCH:
                            U = (D0, D1)[d][:, chunk * P:(chunk + 1) * P]
                        else:
                            U = (D2, D3)[d][:, T + (chunk - SCH) * P:T + (chunk - SCH + 1) * P]
                        return dve.scalar_tensor_tensor(out=S[d][:, dst, :], in0=S[d][:, src, :],
                                                        scalar=EBL[:, d, chunk:chunk + 1], in1=U,
                                                        op0=ALU.mult, op1=ALU.add)

                    dve.wait_ge(u_done, h * 2 + 3)
                    for i in range(SCH - 1):
                        r.add(advance(0, i, i + 1, i))
                        r.add(advance(1, SCH - 1 - i, SCH - 2 - i, SCH - 1 - i))
                        if i < 1:
                            r.add(advance(0, SCH, SCH + 1, SCH))
                            r.add(advance(1, NCH - 1, SCH, NCH - 1))
                        if i == 1:
                            advance(0, SCH + 1, NCH, NCH - 1).then_inc(s_done, 1)
                            advance(1, SCH, NCH, SCH).then_inc(s_done, 1)
                        if i < SCH - 2:
                            r.wait()
                    r.wait()
                    dve.sem_inc(states_done, 1)
                    dve.wait_ge(o_sq, h + 1)
                    r.add(dve.tensor_reduce(SS[:, :], ON[:, :, :], AX.X, ALU.add))
                    r.wait()
                    dve.tensor_scalar(SS[:, :], SS[:, :], 1.0 / P, EPS, ALU.mult, ALU.add).then_inc(ss_done, 1)
                    dve.wait_ge(rt_done, h + 1)
                    r.add(dve.reciprocal(RS[:, :], RT[:, :]))
                    r.wait()
                    r.add(dve.tensor_tensor(ON[:, :, :], D2[:, 0:T].rearrange("p (b v) -> p b v", v=P),
                                            RS[:, :].unsqueeze(2).broadcast_to([P, NB, P]), ALU.mult))
                    r.wait()
                    dve.tensor_tensor(ON[:, :, :], ON[:, :, :], ZG[:, :, :], ALU.mult).then_inc(on_done, 1)
                    dve.wait_ge(on_turned, h + 1)
                    dve.tensor_scalar(YT[:, :, bass.ds(h * P, P)], D3[:, 0:T].rearrange("p (b t) -> p b t", t=P),
                                      gn[:, bass.ds(h, 1)], None, ALU.mult).then_inc(head_done, 1)
                    assert r.n == DSTEPS, r.n

            @block.tensor
            def _(pe):
                pe.sem_inc(proj[3], 1)
                pe.sem_inc(u_done, 1)
                n_pe(pe)
                pe.wait_ge(h_stored, n_stored)
                pe.wait_ge(consts, NCONST)

                def project(dst, w, col):
                    for lo, hi in ((0, LS), (LS, T)):
                        for k in range(KD):
                            last_mm = pe.matmul(dst[:, lo:hi], w[:, k, col * P:(col + 1) * P], HT[:, k, lo:hi],
                                                start=(k == 0), stop=(k == KD - 1))
                    return last_mm

                pe.wait_ge(wfb_in, 16)
                project(D0, wfb, 0).then_inc(proj[0], 1)
                project(D1, wfb, 1).then_inc(proj[1], 1)

                def head(h, final_head):
                    pe.wait_ge(wqvg_in, h * 16 + 16)
                    pe.wait_ge(sig_done, h * 3 + 1)
                    project(D0, wqvg, 0).then_inc(proj[2], 1)
                    pe.wait_ge(sig_done, h * 3 + 2)
                    for b in range(NB):
                        dst = D1[:, b * 2 * P:(b + 1) * 2 * P] if b < SB else D0[:, T:T + 2 * P]
                        if b == SB:
                            pe.wait_ge(q_made, h + 1)
                        for k in range(KD):
                            last = pe.matmul(dst, HT[:, k, b * P:(b + 1) * P], wqvg[:, k, P:3 * P],
                                             start=(k == 0), stop=(k == KD - 1))
                    last.then_inc(proj[3], 1)
                    pe.wait_ge(head_done, h + 1)
                    for d, dst in enumerate((D2, D3)):
                        pe.wait_ge(kl_done, h * 2 + (d + 1))
                        for b in range(NB):
                            last = pe.transpose(dst[:, b * P:(b + 1) * P], KL[d][:, b * P:(b + 1) * P], ident[:, :])
                        last.then_inc(klt_psum, 1)
                    for d, dst in enumerate((D2, D3)):
                        pe.wait_ge(klt_done, h * 2 + (d + 1))
                        for b in range(NB):
                            t = slice(b * P, (b + 1) * P)
                            last = pe.matmul(dst[:, t], KI[d][:, t], QI[d][:, t], start=True, stop=True)
                        last.then_inc(at_psum, 1)
                    pe.wait_ge(vm_done, h * 2 + 2)
                    pe.wait_ge(q_made, h + 1)
                    pe.wait_ge(vg_read, h * 2 + 2)
                    for d, (dst, extra) in enumerate(((D0, D2), (D1, D3))):
                        for b in range(NB):
                            out = dst[:, b * 2 * P:(b + 1) * 2 * P] if b < SB else extra[:, T:T + 2 * P]
                            if b == SB:
                                pe.wait_ge(at_done, h * 2 + (d + 1))
                            last = pe.matmul(out, KLT[d][:, b * P:(b + 1) * P],
                                             Vm[:, b, :, :].rearrange("p c v -> p (c v)"), start=True, stop=True)
                        last.then_inc(u_done, 1)
                    pe.wait_ge(at_done, h * 2 + 2)
                    pe.wait_ge(states_done, h + 1)
                    for b in range(NB):
                        t = slice(b * P, (b + 1) * P)
                        for d in range(2):
                            pe.matmul(D2[:, t], AT[d][:, t], V[:, b, :], start=(d == 0), stop=False,
                                      skip_group_check=True)
                        for half in range(2):
                            c = 2 * b + half
                            for d in range(2):
                                last = pe.matmul(D2[half * CH:(half + 1) * CH, t], QB[d][:, c * CH:(c + 1) * CH],
                                                 S[d][:, c, :], start=False, stop=(d == 1 and half == 1),
                                                 skip_group_check=True)
                    last.then_inc(o_done, 1)
                    if not final_head:
                        pe.wait_ge(wfb_in, h * 16 + 32)
                        project(D0, wfb, 0).then_inc(proj[0], 1)
                    pe.wait_ge(on_done, h + 1)
                    for b in range(NB):
                        last = pe.transpose(D3[:, b * P:(b + 1) * P], ON[:, b, :], ident[:, :])
                    last.then_inc(on_turned, 1)
                    if not final_head:
                        project(D1, wfb, 1).then_inc(proj[1], 1)

                with pe.Fori(0, HG - 1) as h:
                    head(h, False)
                head(HG - 1, True)

    phase(nc, "hgrn", body)


def attention(nc, X, HT, YT, watt, ident, io):
    def body(sb, ps, sem):
        ROT = (2 * NG + 2) * HD
        cos = sb("cos", [P, SB, HD])
        sin = sb("sin", [P, SB, HD])
        QK = sb("QK", [P, NB, ROT])
        TR = sb("TR", [P, 2, ROT])
        VA = sb("VA", [P, NB, P])
        QT = sb("QT", [P, NG + 1, T])
        KT = QT[:, NG, :]
        QG = sb("QG", [P, T])
        CK = sb("CK", [P, P])
        CKT = sb("CKT", [P, P])
        CV = sb("CV", [P, P])
        band = sb("band", [P, 4, P])
        sink = sb("sink", [P, 2, NG])
        LG = sb("LG", [P, 2, 4 * P])
        PR = sb("PR", [P, 2, 4 * P])
        PT = sb("PT", [P, 2, 4 * P])
        mx = sb("mx", [P, 2 * NB])
        nm = sb("nm", [P, 2 * NB])
        den = sb("den", [P, 2 * NB])
        es = sb("es", [P, 2 * NB])
        rd = sb("rd", [P, 2 * NB])
        A = [ps(f"A{i}", 1024) for i in range(4)]
        L = [A[0][:, 0:512], A[0][:, 512:1024]]
        TP = [A[1][:, 0:512], A[1][:, 512:1024]]
        O = A[2]

        tables_in, ctx_in, sink_in, kv_out = sem("tables_in"), sem("ctx_in"), sem("sink_in"), sem("kv_out")
        mask_step, projected, evacuated = sem("mask_step"), sem("projected"), sem("evacuated")
        turned, t_stored, raw_k = sem("a_turned"), sem("a_stored"), sem("raw_k")
        rot_step, v_stored = sem("rot_step"), sem("v_stored")
        g_staged, lg_done, nm_done, exp_done = sem("g_staged"), sem("lg_done"), sem("nm_done"), sem("a_exp")
        pn_done, tp_done, pt_done, pv_done, o_stored = (sem(n) for n in ("pn_done", "tp_done", "pt_done", "pv_done", "o_stored"))
        astep = sem("astep")
        U = 2 * NB

        def spans(b):
            if b == SB:
                return [(2, KT[:, SB * P:T])]
            out = [(1, CKT[:, :])]
            if b > 0:
                out.insert(0, (0, KT[:, (b - 1) * P:b * P]))
            hi = min(b + 2, SB)
            out.append((2, KT[:, b * P:hi * P]))
            return out

        def columns(b):
            if b == SB:
                return 2, 3
            return (0 if b else 1), (4 if b < SB - 1 else 3)

        def values(b, n):
            if b == SB:
                return VA[:, SB, :]
            return CV[:, :] if n == 1 else VA[:, b + (-1, 0, 0, 1)[n], :]

        with nc.Block() as block:
            @block.sync
            def _(sp):
                sp.dma_start(cos[:, :, :], io["rope_cos"]).then_inc(tables_in, 16)
                sp.dma_start(sin[:, :, :], io["rope_sin"]).then_inc(tables_in, 16)
                sp.dma_start(CK[:, :], io["cache_k"].rearrange("b n s k d -> (b n s) (k d)")).then_inc(ctx_in, 16)
                sp.dma_start(CV[:, :], io["cache_v"].rearrange("b n s k d -> (b n s) (k d)")).then_inc(ctx_in, 16)
                sp.dma_start(sink[:, :, :].rearrange("p a g -> p (a g)"),
                             broadcast_rows(io["attn_sink"].rearrange("n h -> (n h)"), 0, 2 * NG)).then_inc(sink_in, 16)
                sp.wait_ge(raw_k, 1)
                sp.dma_start(io["new_k"].rearrange("b n s k d -> (b n s) (k d)"), QK[:, SB, 2 * NG * HD:ROT]).then_inc(kv_out, 16)
                sp.wait_ge(v_stored, NB)
                sp.dma_start(io["new_v"].rearrange("b n s k d -> (b n s) (k d)"), VA[:, SB, :]).then_inc(kv_out, 16)
                sp.wait_ge(kv_out, 32)

            @block.gpsimd
            def _(pool):
                pool.memset(band[:, :, :], 0.0).then_inc(mask_step, 1)
                pool.wait_ge(mask_step, 1)
                pool.affine_select(out=band[:, 0, :], in_=band[:, 0, :], compare_op=ALU.is_ge, fill=NEG,
                                   base=0, pattern=[[1, P]], channel_multiplier=-1).then_inc(mask_step, 1)
                pool.affine_select(out=band[:, 3, :], in_=band[:, 3, :], compare_op=ALU.is_ge, fill=NEG,
                                   base=0, pattern=[[-1, P]], channel_multiplier=1).then_inc(mask_step, 1)

            @block.scalar
            def _(act):
                act.wait_ge(projected, NB)
                act.activation(QK[:, SB, :], A[SB % 2][:, 0:ROT], ACT.Copy).then_inc(raw_k, 1)
                act.activation(VA[:, SB, :], A[SB % 2][:, ROT:ROT + P], ACT.Copy).then_inc(v_stored, 1)
                for b in range(NB):
                    act.wait_ge(turned, b + 1)
                    act.activation(QT[:, :, b * P:(b + 1) * P],
                                   A[2 + b % 2][:, 0:(NG + 1) * P].rearrange("p (g t) -> p g t", t=P), ACT.Copy).then_inc(t_stored, 1)
                act.wait_ge(turned, NB + 1)
                act.activation(CKT[:, :], A[2 + NB % 2][:, 0:P], ACT.Copy).then_inc(t_stored, 1)
                act.wait_ge(t_stored, NB + 1)
                act.wait_ge(sink_in, 16)
                act.sem_inc(o_stored, 1)
                with act.Fori(0, NG) as g:
                    act.wait_ge(pv_done, g * U + 1)
                    act.activation(QG[:, :], QT[:, bass.ds(g, 1), :].rearrange("p a t -> p (a t)"), ACT.Copy).then_inc(g_staged, 1)
                    for s in range(U + 1):
                        if s < U:
                            b, kv = divmod(s, 2)
                            lo, hi = columns(b)
                            c = slice(lo * P, hi * P)
                            act.wait_ge(nm_done, g * U + (s + 1))
                            act.activation(PR[:, s % 2, c], LG[:, s % 2, c], ACT.Exp, bias=nm[:, s:s + 1],
                                           accum_out=den[:, s:s + 1])
                            act.activation(es[:, s:s + 1], sink[:, kv, bass.ds(g, 1)], ACT.Exp,
                                           bias=nm[:, s:s + 1]).then_inc(exp_done, 1)
                        if s >= 1:
                            lo, hi = columns((s - 1) // 2)
                            c = slice(lo * P, hi * P)
                            act.wait_ge(tp_done, g * U + s)
                            act.activation(PT[:, (s - 1) % 2, c], TP[(s - 1) % 2][:, c], ACT.Copy).then_inc(pt_done, 1)
                    act.wait_ge(pv_done, g * U + (U + 1))
                    act.activation(YT[:, :, bass.ds(g * P + HG * P, P)],
                                   O[:, 0:T].rearrange("p (b t) -> p b t", t=P), ACT.Copy).then_inc(o_stored, 1)

            @block.vector
            def _(dve):
                dve.wait_ge(tables_in, 32)
                r = Count(dve, rot_step)
                for b in range(SB):
                    dve.wait_ge(projected, b + 1)
                    z = A[b % 2][:, 0:ROT]
                    n = ROT // HD
                    head = lambda t: t.rearrange("p (n d) -> p n d", d=HD)
                    quarter = lambda t: t.rearrange("p (n a w f) -> p n a w f", a=2, w=2, f=HD // 4)
                    table = lambda t: t[:, b, :].unsqueeze(1).broadcast_to([P, n, HD])
                    r.add(dve.tensor_tensor(head(TR[:, 0, :]), head(z), table(cos), ALU.mult))
                    for w in range(2):
                        sn = sin[:, b, :].rearrange("p (a w f) -> p a w f", a=2, w=2)[:, :, w, :]
                        r.add(dve.tensor_tensor(quarter(TR[:, 1, :])[:, :, :, w, :], quarter(z)[:, :, :, 1 - w, :],
                                                sn.unsqueeze(1).broadcast_to([P, n, 2, HD // 4]), ALU.mult))
                    dve.tensor_copy(VA[:, b, :], A[b % 2][:, ROT:ROT + P]).then_inc(v_stored, 1)
                    r.wait()
                    dve.tensor_tensor(QK[:, b, :], TR[:, 0, :], TR[:, 1, :], ALU.add).then_inc(evacuated, 1)
                    dve.wait_ge(evacuated, b + 1)
                dve.wait_ge(mask_step, 3)
                dve.wait_ge(sink_in, 16)
                with dve.Fori(0, NG) as g:
                    r = Count(dve, astep, g * (3 * U))
                    for s in range(U + 1):
                        if s < U:
                            b, kv = divmod(s, 2)
                            lo, hi = columns(b)
                            c = slice(lo * P, hi * P)
                            wait_apart(dve, lg_done, g * U + (s + 1))
                            r.add(dve.tensor_tensor_reduce(LG[:, s % 2, c], L[kv][:, c],
                                                           band[:, :, :].rearrange("p a k -> p (a k)")[:, c],
                                                           SCALE, -3e38, ALU.add, ALU.max, mx[:, s:s + 1]))
                            r.wait()
                            dve.tensor_scalar(nm[:, s:s + 1], mx[:, s:s + 1], sink[:, kv, bass.ds(g, 1)], -1.0,
                                              ALU.max, ALU.mult).then_inc(nm_done, 1)
                        if s >= 1:
                            q = s - 1
                            lo, hi = columns(q // 2)
                            c = slice(lo * P, hi * P)
                            dve.wait_ge(exp_done, g * U + s)
                            r.add(dve.tensor_tensor(rd[:, q:q + 1], den[:, q:q + 1], es[:, q:q + 1], ALU.add))
                            r.wait()
                            r.add(dve.reciprocal(rd[:, q:q + 1], rd[:, q:q + 1]))
                            r.wait()
                            dve.tensor_scalar(PR[:, q % 2, c], PR[:, q % 2, c], rd[:, q:q + 1], None,
                                              ALU.mult).then_inc(pn_done, 1)
                    assert r.n == 3 * U

            @block.tensor
            def _(pe):
                for b in range(NB):
                    if b >= 2:
                        pe.wait_ge(evacuated, b - 1)
                        pe.wait_ge(v_stored, b - 1)
                    for lo, hi in ((0, 512), (512, ROT + P)):
                        for k in range(KD):
                            last = pe.matmul(A[b % 2][:, lo:hi], HT[:, k, b * P:(b + 1) * P], watt[:, k, lo:hi],
                                             start=(k == 0), stop=(k == KD - 1))
                    last.then_inc(projected, 1)
                pe.wait_ge(ctx_in, 32)
                for b in range(NB):
                    if b < SB:
                        pe.wait_ge(evacuated, b + 1)
                    else:
                        pe.wait_ge(raw_k, 1)
                    if b >= 2:
                        pe.wait_ge(t_stored, b - 1)
                    for i in range(NG + 1):
                        last = pe.transpose(A[2 + b % 2][:, i * P:(i + 1) * P], QK[:, b, i * P:(i + 1) * P], ident[:, :])
                    last.then_inc(turned, 1)
                pe.wait_ge(t_stored, NB - 1)
                pe.transpose(A[2 + NB % 2][:, 0:P], CK[:, :], ident[:, :]).then_inc(turned, 1)
                pe.wait_ge(t_stored, NB + 1)
                pe.wait_ge(v_stored, NB)
                pe.sem_inc(pv_done, 1)
                with pe.Fori(0, NG) as g:
                    pe.wait_ge(g_staged, g + 1)

                    def logits(s):
                        b, kv = divmod(s, 2)
                        rows = slice(kv * HD, (kv + 1) * HD)
                        if s >= 2:
                            pe.wait_ge(nm_done, g * U + (s - 1))
                        for n, keys in spans(b):
                            cols = keys.shape[1]
                            last = pe.matmul(L[kv][:, n * P:n * P + cols], QG[rows, b * P:(b + 1) * P], keys[rows, :],
                                             start=True, stop=True)
                        last.then_inc(lg_done, 1)

                    logits(0)
                    logits(1)
                    for s in range(1, U + 2):
                        if s + 1 < U:
                            logits(s + 1)
                        if s <= U:
                            q = s - 1
                            pe.wait_ge(pn_done, g * U + s)
                            for n in range(*columns(q // 2)):
                                last = pe.transpose(TP[q % 2][:, n * P:(n + 1) * P], PR[:, q % 2, n * P:(n + 1) * P], ident[:, :])
                            last.then_inc(tp_done, 1)
                        if s >= 2:
                            q = s - 2
                            b, kv = divmod(q, 2)
                            pe.wait_ge(pt_done, g * U + (q + 1))
                            if q == 0:
                                pe.wait_ge(o_stored, g + 1)
                            lo, hi = columns(b)
                            for n in range(lo, hi):
                                last = pe.matmul(O[kv * HD:(kv + 1) * HD, b * P:(b + 1) * P],
                                                 values(b, n)[:, kv * HD:(kv + 1) * HD], PT[:, q % 2, n * P:(n + 1) * P],
                                                 start=(n == lo), stop=(n == hi - 1))
                            last.then_inc(pv_done, 1)

    phase(nc, "att", body)


def even_mixer(nc, X, HT, YT, ident, io):
    with ExitStack() as ctx:
        watt = ctx.enter_context(nc.sbuf_tensor("watt", [P, KD, 6 * P], F32))
        hgrn(nc, X, HT, YT, watt, ident, io)
        attention(nc, X, HT, YT, watt, ident, io)


def rglru(nc, HT, YT, ident, io):
    def body(sb, ps, sem):
        NPAR, NCOL = 13, 17
        TAPS, CB, BA, BX, LAM, H0, CA, CT = 0, 4, 5, 7, 9, 11, 13, 15
        W = KD // RB
        XP = T + 6
        w = sb("wlru", [P, KD, 4 * P])
        wrg = sb("wrg", [P, W, 4, W * P])
        chan = sb("chan", [P, KD, NCOL])
        par = sb("par", [P, W, NCOL])
        sp_y = sb("sp_y", [P, KD, 2])
        sp_m = sb("sp_m", [P, KD, 2])
        sp_z = sb("sp_z", [P, KD, 2])
        sp_s = sb("sp_s", [P, KD, 2])
        sp_p = sb("sp_p", [P, KD, 2])
        ends = sb("ends", [P, 2, KD])
        endsT = sb("endsT", [2 * KD, P])
        xp = [sb(f"xp{c}", [P, XP]) for c in range(W)]
        cv = [sb(f"cv{c}", [P, T + 3]) for c in range(W)]
        xc = [sb(f"xc{c}", [P, T]) for c in range(W)]
        GT = [sb(f"GT{c}", [P, T]) for c in range(W)]
        R, I, AA, HH = ([[sb(f"{n}{d}{c}", [P, T]) for c in range(W)] for d in range(2)] for n in ("R", "I", "AA", "HH"))
        Dp = [ps(f"D{i}", 1024) for i in range(4)]

        chan_in = sem("chan_in")
        pads, sp_step, sp_exp, sp_ready = sem("pads"), sem("sp_step"), sem("sp_exp"), sem("sp_ready")
        w_in, wrg_in = sem("wlru_in"), sem("wrg_in")
        xr_done, gt_done, rg_done = sem("xr_done"), sem("gt_done"), sem("rg_done")
        xp_done, gelu_done, sig_done, ex_done, sq_done = (sem(n) for n in ("xp_done", "gelu_done", "l_sig", "l_ex", "sq_done"))
        conv_done, m_done, y_done, lstep = sem("conv_done"), sem("m_done"), sem("l_y"), sem("lstep")
        ends_turned, ends_stored, ends_out = sem("ends_turned"), sem("ends_stored"), sem("ends_out")
        LSTEPS = 1 + W * 3 + 2 * W * 2 + 2 * W * 2 + 2 * W * 2 + W

        with nc.Block() as block:
            @block.sync
            def _(sp):
                sp.dma_start(chan[:, :, 0:NPAR], io["channels"]).then_inc(chan_in, 16)
                with sp.Fori(0, RB) as n:
                    sp.wait_ge(gt_done, n * W + 1)
                    sp.dma_start(w[:, :, :].rearrange("p k n -> p (k n)"),
                                 io["w_lru"][bass.ds(n, 1), :, :].rearrange("a p n -> (a p) n")).then_inc(w_in, 16)
                    sp.wait_ge(rg_done, n * (4 * W) + 1)
                    sp.dma_start(wrg[:, :, :, :].rearrange("p k m n -> p (k m n)"),
                                 io["w_rg"][bass.ds(n, 1), :, :].rearrange("a p n -> (a p) n")).then_inc(wrg_in, 16)
                sp.wait_ge(ends_stored, 1)
                for d, name in enumerate(("new_lf", "new_lb")):
                    sp.dma_start(io[name].rearrange("b n (k p) -> (b n k) p", p=P), endsT[d * KD:(d + 1) * KD, :]).then_inc(ends_out, 16)
                sp.wait_ge(ends_out, 32)

            @block.gpsimd
            def _(pool):
                for c in range(W):
                    for lo, hi in ((0, 2), (LS + 2, LS + 5), (XP - 1, XP)):
                        pool.memset(xp[c][:, lo:hi], 0.0).then_inc(pads, 1)

            @block.scalar
            def _(act):
                act.wait_ge(sp_step, 3)
                act.activation(sp_y[:, :, :], sp_y[:, :, :], ACT.Exp, scale=-1.0).then_inc(sp_exp, 1)
                with act.Fori(0, RB) as n:
                    for c in range(W):
                        act.wait_ge(xr_done, n * W + (c + 1))
                        act.activation(xp[c][:, 2:LS + 2], Dp[c][:, 0:LS], ACT.Copy)
                        act.activation(xp[c][:, LS + 5:XP - 1], Dp[c][:, LS:T], ACT.Copy).then_inc(xp_done, 1)
                    act.wait_ge(y_done, n * W + 1)
                    for c in range(W):
                        act.wait_ge(gt_done, n * W + (c + 2))
                        act.activation(GT[c][:, :], Dp[2 + c][:, 0:T], ACT.Gelu_apprx_tanh).then_inc(gelu_done, 1)
                    act.wait_ge(conv_done, n * W + W)
                    i = 0
                    for d in range(2):
                        for c in range(W):
                            for dst, bias in ((R, BA), (I, BX)):
                                act.wait_ge(rg_done, n * (4 * W) + (i + 2))
                                act.activation(dst[d][c][:, :], Dp[i % 4][:, 0:T], ACT.Sigmoid,
                                               bias=par[:, c, bias + d:bias + d + 1]).then_inc(sig_done, 1)
                                i += 1
                    act.wait_ge(sig_done, n * (4 * W) + (4 * W + 1))
                    for d in range(2):
                        for c in range(W):
                            act.activation(AA[d][c][:, :], R[d][c][:, :], ACT.Exp, scale=par[:, c, CA + d:CA + d + 1])
                            act.activation(R[d][c][:, :], R[d][c][:, :], ACT.Tanh,
                                           scale=par[:, c, CT + d:CT + d + 1]).then_inc(ex_done, 1)
                    for d in range(2):
                        for c in range(W):
                            act.wait_ge(m_done, n * (2 * W) + (d * W + c + 1))
                            act.activation(R[d][c][:, :], R[d][c][:, :], ACT.Sqrt).then_inc(sq_done, 1)
                act.wait_ge(ends_turned, 1)
                act.activation(endsT[:, :], Dp[0][0:2 * KD, 0:P], ACT.Copy).then_inc(ends_stored, 1)

            @block.vector
            def _(dve):
                dve.sem_inc(y_done, 1)
                c = Count(dve, sp_step)
                lam = chan[:, :, LAM:LAM + 2]
                dve.wait_ge(chan_in, 16)
                c.add(dve.tensor_scalar(sp_s[:, :, :], lam, -1.0, None, ALU.mult))
                c.wait()
                c.add(dve.tensor_scalar(sp_m[:, :, :], sp_s[:, :, :], 0.0, None, ALU.max))
                c.add(dve.tensor_tensor(sp_y[:, :, :], lam, sp_s[:, :, :], ALU.max))
                dve.wait_ge(sp_exp, 1)
                c.add(dve.tensor_scalar(sp_z[:, :, :], sp_y[:, :, :], 2.0, None, ALU.add))
                c.wait()
                c.add(dve.reciprocal(sp_z[:, :, :], sp_z[:, :, :]))
                c.wait()
                c.add(dve.tensor_tensor(sp_z[:, :, :], sp_z[:, :, :], sp_y[:, :, :], ALU.mult))
                c.wait()
                c.add(dve.tensor_tensor(sp_s[:, :, :], sp_z[:, :, :], sp_z[:, :, :], ALU.mult))
                c.wait()
                c.add(dve.tensor_scalar(sp_p[:, :, :], sp_s[:, :, :], 1.0 / 19, None, ALU.mult))
                for k in range(17, 1, -2):
                    c.wait()
                    c.add(dve.scalar_tensor_tensor(out=sp_p[:, :, :], in0=sp_p[:, :, :], scalar=1.0 / k, in1=sp_s[:, :, :],
                                                   op0=ALU.add, op1=ALU.mult))
                c.wait()
                c.add(dve.scalar_tensor_tensor(out=sp_p[:, :, :], in0=sp_p[:, :, :], scalar=1.0, in1=sp_z[:, :, :],
                                               op0=ALU.add, op1=ALU.mult))
                c.wait()
                c.add(dve.scalar_tensor_tensor(out=sp_p[:, :, :], in0=sp_p[:, :, :], scalar=2.0, in1=sp_m[:, :, :],
                                               op0=ALU.mult, op1=ALU.add))
                c.wait()
                dve.tensor_scalar(chan[:, :, CA:CA + 2], sp_p[:, :, :], -8.0, None, ALU.mult).then_inc(sp_ready, 1)
                dve.tensor_scalar(chan[:, :, CT:CT + 2], sp_p[:, :, :], 8.0, None, ALU.mult).then_inc(sp_ready, 1)
                dve.wait_ge(sp_ready, 2)
                dve.wait_ge(pads, 3 * W)
                with dve.Fori(0, RB) as n:
                    r = Count(dve, lstep, n * LSTEPS)
                    r.add(dve.tensor_copy(par[:, :, :], chan[:, bass.ds(n * W, W), :]))
                    r.wait()
                    for c in range(W):
                        dve.wait_ge(xp_done, n * W + (c + 1))
                        r.add(dve.tensor_scalar(cv[c][:, :], xp[c][:, 0:T + 3], par[:, c, TAPS:TAPS + 1],
                                                par[:, c, CB:CB + 1], ALU.mult, ALU.add))
                        r.wait()
                        for tap in (1, 2):
                            r.add(dve.scalar_tensor_tensor(out=cv[c][:, :], in0=xp[c][:, tap:tap + T + 3],
                                                           scalar=par[:, c, TAPS + tap:TAPS + tap + 1], in1=cv[c][:, :],
                                                           op0=ALU.mult, op1=ALU.add))
                            r.wait()
                        for lo, hi, at in ((0, LS, 0), (LS, T, 3)):
                            last = dve.scalar_tensor_tensor(out=xc[c][:, lo:hi], in0=xp[c][:, lo + at + 3:hi + at + 3],
                                                            scalar=par[:, c, TAPS + 3:TAPS + 4], in1=cv[c][:, lo + at:hi + at],
                                                            op0=ALU.mult, op1=ALU.add)
                        last.then_inc(conv_done, 1)
                    dve.wait_ge(conv_done, n * W + W)
                    for d in range(2):
                        for c in range(W):
                            dve.wait_ge(ex_done, n * (2 * W) + (d * W + c + 1))
                            r.add(dve.tensor_tensor(HH[d][c][:, :], AA[d][c][:, :], AA[d][c][:, :], ALU.mult))
                            r.add(dve.tensor_tensor(I[d][c][:, :], I[d][c][:, :], xc[c][:, :], ALU.mult))
                            r.wait()
                            dve.scalar_tensor_tensor(out=R[d][c][:, :], in0=HH[d][c][:, :], scalar=1.0, in1=R[d][c][:, :],
                                                     op0=ALU.add, op1=ALU.mult).then_inc(m_done, 1)
                    for d in range(2):
                        for c in range(W):
                            dve.wait_ge(sq_done, n * (2 * W) + (d * W + c + 1))
                            r.add(dve.tensor_tensor(I[d][c][:, :], I[d][c][:, :], R[d][c][:, :], ALU.mult))
                            r.wait()
                            for k, (lo, hi, h0) in enumerate(((0, LS, par[:, c, H0 + d:H0 + d + 1]), (LS, T, 0.0))):
                                t = slice(hi - 1, lo - 1 if lo else None, -1) if d else slice(lo, hi)
                                ins = dve.tensor_tensor_scan(HH[d][c][:, t], AA[d][c][:, t], I[d][c][:, t], h0,
                                                             ALU.mult, ALU.add)
                                r.add(ins)
                            r.wait()
                            end = LS if d else T - 1
                            r.add(dve.tensor_copy(ends[:, d, bass.ds(n * W + c, 1)], HH[d][c][:, end:end + 1]))
                    for c in range(W):
                        r.add(dve.tensor_tensor(HH[0][c][:, :], HH[0][c][:, :], HH[1][c][:, :], ALU.add))
                    r.wait()
                    dve.wait_ge(gelu_done, n * W + W)
                    for c in range(W):
                        dve.tensor_tensor(YT[:, :, bass.ds((n * W + c) * P, P)],
                                          HH[0][c][:, :].rearrange("p (b t) -> p b t", t=P),
                                          GT[c][:, :].rearrange("p (b t) -> p b t", t=P), ALU.mult).then_inc(y_done, 1)
                    assert r.n == LSTEPS, r.n

            @block.tensor
            def _(pe):
                for s in (gt_done, rg_done, sig_done):
                    pe.sem_inc(s, 1)
                with pe.Fori(0, RB) as n:
                    pe.wait_ge(w_in, n * 16 + 16)
                    pe.wait_ge(sig_done, n * (4 * W) + 1)
                    for part, done in ((0, xr_done), (1, gt_done)):
                        for c in range(W):
                            for lo, hi in ((0, LS), (LS, T)):
                                for k in range(KD):
                                    last = pe.matmul(Dp[2 * part + c][:, lo:hi], w[:, k, (part * W + c) * P:(part * W + c + 1) * P],
                                                     HT[:, k, lo:hi], start=(k == 0), stop=(k == KD - 1))
                            last.then_inc(done, 1)
                    pe.wait_ge(wrg_in, n * 16 + 16)
                    pe.wait_ge(conv_done, n * W + W)
                    i = 0
                    for d in range(2):
                        for c in range(W):
                            for ax in range(2):
                                if i == 2:
                                    pe.wait_ge(gelu_done, n * W + W)
                                if i >= 4:
                                    pe.wait_ge(sig_done, n * (4 * W) + (i - 4 + 2))
                                for lo, hi in ((0, LS), (LS, T)):
                                    for k in range(W):
                                        last = pe.matmul(Dp[i % 4][:, lo:hi], wrg[:, k, 2 * d + ax, c * P:(c + 1) * P],
                                                         xc[k][:, lo:hi], start=(k == 0), stop=(k == W - 1))
                                last.then_inc(rg_done, 1)
                                i += 1
                pe.wait_ge(lstep, RB * LSTEPS)
                pe.wait_ge(sig_done, RB * 4 * W + 1)
                pe.transpose(Dp[0][0:2 * KD, 0:P], ends[:, :, :].rearrange("p d k -> p (d k)"), ident[:, :]).then_inc(ends_turned, 1)

    phase(nc, "lru", body)


def build(nc, io):
    with ExitStack() as ctx:
        X = ctx.enter_context(nc.sbuf_tensor("X", [P, NB, D], F32))
        ident = ctx.enter_context(nc.sbuf_tensor("ident", [P, P], F32))
        iota16 = ctx.enter_context(nc.sbuf_tensor("iota16", [P, TOPK], F32))
        HY = ctx.enter_context(nc.sbuf_tensor("HY", [P, NB, D], F32))
        HT = ctx.enter_context(nc.sbuf_tensor("HT", [P, KD, T], F32))
        constants(nc, iota16)
        modulation(nc, X, HY, HT, ident, io)
        even_mixer(nc, X, HT, HY, ident, io)
        project_and_peer(nc, X, HY, HT, ident, iota16, 0, io)
        rglru(nc, HT, HY, ident, io)
        project_and_peer(nc, X, HY, HT, ident, iota16, 1, io)


def constants(nc, iota16):
    with nc.Block() as block:
        @block.gpsimd
        def _(pool):
            pool.iota(iota16[:, :], pattern=[[1, TOPK]], base=0, channel_multiplier=0,
                      allow_small_or_imprecise_dtypes=True)


def lay_out(a):
    def tiles(w, n):
        k, cols = w.shape
        return np.ascontiguousarray(w.reshape(k // P, P, cols // n, n).transpose(2, 1, 0, 3)).reshape(cols // n, P, -1)

    out = {k: a[k] for k in ("x_prompt", "x_sample", "b_mod", "norm1_g", "norm2_g", "final_g", "cache_k", "cache_v",
                             "attn_sink")}
    w = a["w_in_even"][0]
    n = HG * P
    for name, parts in (("w_hgrn_fb", (1, 2)), ("w_hgrn_qvg", (0, 3, 4))):
        out[name] = np.stack([tiles(np.concatenate([w[:, s * n + h * P:s * n + (h + 1) * P] for s in parts], axis=1),
                                    len(parts) * P)[0] for h in range(HG)])
    wq = w[:, 5 * n:5 * n + 2 * NG * HD].reshape(D, 2, NG, HD).transpose(0, 2, 1, 3).reshape(D, -1)
    out["w_att"] = tiles(np.concatenate([wq, w[:, 5 * n + 2 * NG * HD:]], axis=1), 6 * P)[0]
    wo = a["w_out_even"][0]
    wo = np.concatenate([wo[:n], wo[n:].reshape(2, NG, HD, D).transpose(1, 0, 2, 3).reshape(-1, D)])
    out["w_out"] = np.stack([wo, a["w_out_odd"][0]])
    lb = np.stack([a["hgrn_lb_fwd"], a["hgrn_lb_bwd"]])
    out["hgrn_lb"] = np.ascontiguousarray(lb.reshape(2, 2, HG, P).transpose(3, 0, 1, 2))
    out["gnormT"] = np.ascontiguousarray(a["hgrn_gnorm_g"].reshape(HG, P).T)
    out["state0"] = np.stack([a["state_hgrn_fwd"][0, 0], a["state_hgrn_bwd"][0, 0]])
    ch = np.concatenate([a["conv_w"][0], a["conv_b"], a["rg_b_a"][0], a["rg_b_x"][0], a["rg_lambda"][0],
                         a["state_lru_fwd"][0], a["state_lru_bwd"][0]])
    out["channels"] = np.ascontiguousarray(ch.reshape(13, KD, P).transpose(2, 1, 0))
    wi = a["w_in_odd"][0]
    out["w_lru"] = np.stack([tiles(np.concatenate([wi[:, D + n * 256:D + (n + 1) * 256], wi[:, n * 256:(n + 1) * 256]],
                                                  axis=1), 4 * P)[0] for n in range(RB)])
    rg = np.stack([a["rg_w_a"][0], a["rg_w_x"][0]], axis=1)
    out["w_rg"] = np.ascontiguousarray(rg.reshape(4, RB, 2, P, 256).transpose(1, 3, 2, 0, 4)).reshape(RB, P, -1)
    t = np.arange(LS)
    inv = (1.0 / (np.float32(10000.0) ** (np.arange(HD // 4, dtype=np.float32) / np.float32(HD // 4)))).astype(np.float32)
    pos = np.stack([t // 64, t % 64], axis=1).astype(np.float32)
    ang = pos[:, :, None] * inv
    cos = np.stack([np.cos(ang)] * 2, axis=2)
    sin = np.stack([-np.sin(ang), np.sin(ang)], axis=2)
    for name, table in (("rope_cos", cos), ("rope_sin", sin)):
        out[name] = np.ascontiguousarray(table.reshape(SB, P, HD).transpose(1, 0, 2)).astype(np.float32)
    cond = np.stack([a["c"][0], a["c_ctx"]])
    out["condT"] = np.ascontiguousarray(cond.reshape(2, KD, P).transpose(2, 1, 0))
    out["w_mod"] = np.concatenate([tiles(a["w_mod"][l], 512) for l in range(LAYERS)])
    out["w_q"] = np.concatenate([tiles(a["peer_w_q"][l], 2 * P) for l in range(LAYERS)])
    out["keysT"] = np.ascontiguousarray(a["peer_keys"].transpose(0, 2, 4, 1, 3)).reshape(LAYERS * HEADS, P, 2 * NK)
    out["uv"] = np.concatenate([a["peer_u"], a["peer_v"]], axis=2).reshape(LAYERS * EXPERTS, 2 * D)
    return out


OUTS = [("y_prompt", (1, LP, D)), ("y_sample", (1, LS, D)), ("new_k", (1, 1, LP, 2, HD)), ("new_v", (1, 1, LP, 2, HD)),
        ("new_hf", (1, 1, HG, P, P)), ("new_hb", (1, 1, HG, P, P)), ("new_lf", (1, 1, D)), ("new_lb", (1, 1, D))]


def kernel(**inputs):
    import concourse.bacc as bacc
    from concourse.bass_utils import run_bass_kernel_spmd

    nc = bacc.Bacc("TRN2", target_bir_lowering=False, num_devices=1)
    arrays = lay_out({k: np.asarray(v) for k, v in inputs.items()})
    io, given = {}, {}
    for name, a in arrays.items():
        given["in_" + name] = a
        io[name] = nc.dram_tensor("in_" + name, a.shape, mybir.dt.from_np(a.dtype), kind="ExternalInput").ap()
    for name, shape in OUTS:
        io[name] = nc.dram_tensor("out_" + name, shape, F32, kind="ExternalOutput").ap()
    io["mod_rows"] = nc.dram_tensor("scratch_mod_rows", (2 * LAYERS * 6 * D,), F32, kind="Internal").ap()
    build(nc, io)
    r = run_bass_kernel_spmd(nc, [given], core_ids=[0])
    return tuple(r.results[0]["out_" + name] for name, _ in OUTS)
```
